# Optimizing a Trainium2 kernel written in Bass

```python
import jax, jax.numpy as jnp
from jax import lax
import numpy as np

D_MODEL = 1024
BATCH = 1
SEQ = 256
DEPTH = 2
DEC_BATCH = 8
DEC_SEQ = 4
PAST_LEN = 2048
PAGE_SIZE = 128

D_MIX = D_MODEL
D_A = D_MIX // 4
D_B = D_MIX // 4
D_C = D_MIX // 4
D_D = D_MIX - D_A - D_B - D_C
CONV_A_W = 31
CONV_C_W = 3
CHUNK = 128
N_HEADS_B = 4
HD_B = D_B // N_HEADS_B
POOL_WINDOWS = (2, 4, 8, 16)
N_POOL_GROUPS = 4
POOL_GC = D_D // N_POOL_GROUPS
POOL_PAST = 15
D_IN = 2 * D_A + 2 * D_B + 3 * D_C + D_D
SPLIT_POINTS = (D_A, 2 * D_A, 2 * D_A + D_B, 2 * D_A + 2 * D_B, 2 * D_A + 2 * D_B + D_C,
                2 * D_A + 2 * D_B + 2 * D_C, 2 * D_A + 2 * D_B + 3 * D_C)
D_FF = (7 * D_MODEL) // 2
N_EXPERTS = 8
TOP_K = 2
MOE_BLOCK = 128
N_DENSE = (DEPTH + 1) // 2
N_MOE = DEPTH // 2
ALPHA = (2.0 * DEPTH) ** 0.25
BETA = (8.0 * DEPTH) ** -0.25
LN_EPS = 1e-5

kernel_name = "hymba_conv_gmlp_pool_deepnorm_decode"

def layer_norm(x, g, b):
    xf = x.astype(jnp.float32)
    mu = jnp.mean(xf, axis=-1, keepdims=True)
    var = jnp.mean(jnp.square(xf - mu), axis=-1, keepdims=True)
    return ((xf - mu) * lax.rsqrt(var + LN_EPS) * g + b).astype(x.dtype)

def causal_depthwise_conv(past, cur, w):
    width, ch = w.shape
    ext = jnp.concatenate([past, cur], axis=1)
    y = lax.conv_general_dilated(ext, w[:, None, :].astype(ext.dtype), window_strides=(1,),
                                 padding='VALID', dimension_numbers=('NWC', 'WIO', 'NWC'),
                                 feature_group_count=ch)
    return y, ext[:, ext.shape[1] - (width - 1):]

def chunk_gmlp(u, v, w_s, b_s):
    bsz, L, _ = v.shape
    n_chunks = -(-L // CHUNK)
    pad = n_chunks * CHUNK - L
    vp = jnp.pad(v, ((0, 0), (0, pad), (0, 0))).reshape(bsz, n_chunks, CHUNK, N_HEADS_B, HD_B)
    mask = jnp.tril(jnp.ones((CHUNK, CHUNK), dtype=bool))
    ws = jnp.where(mask[None], w_s, 0)
    s = jnp.einsum('hij,bcjhd->bcihd', ws, vp) + jnp.transpose(b_s)[None, None, :, :, None]
    s = s.reshape(bsz, n_chunks * CHUNK, D_B)[:, :L]
    return u * s

def pool_mixer(past, cur, w_pool, scale, start_pos):
    bsz, L, _ = cur.shape
    ext = jnp.concatenate([past, cur], axis=1)
    cs = jnp.pad(jnp.cumsum(ext.astype(jnp.float32), axis=1), ((0, 0), (1, 0), (0, 0)))
    end = cs[:, POOL_PAST + 1:]
    pos = (start_pos + jnp.arange(L)).astype(jnp.float32)
    means = []
    for g, w in enumerate(POOL_WINDOWS):
        sl = slice(g * POOL_GC, (g + 1) * POOL_GC)
        start = cs[:, POOL_PAST + 1 - w:POOL_PAST + 1 - w + L, sl]
        count = jnp.minimum(pos + 1.0, float(w))[None, :, None]
        means.append((end[..., sl] - start) / count)
    mean = jnp.concatenate(means, axis=-1)
    d = (mean - cur.astype(jnp.float32)).astype(cur.dtype).reshape(bsz, L, N_POOL_GROUPS, POOL_GC)
    y = jnp.einsum('blgc,gcd->blgd', d, w_pool).reshape(bsz, L, D_D) * scale
    return y, ext[:, ext.shape[1] - POOL_PAST:]

def dense_swiglu(h, w_gate, w_up, w_down):
    return (jax.nn.silu(h @ w_gate) * (h @ w_up)) @ w_down

def moe_swiglu(h, w_router, w_gate, w_up, w_down):
    T, D = h.shape
    logits = (h @ w_router).astype(jnp.float32)
    top_logit, top_e = lax.top_k(logits, TOP_K)
    gates = jax.nn.softmax(top_logit, axis=-1).astype(h.dtype)
    n_assign = T * TOP_K
    flat_e = top_e.reshape(-1)
    order = jnp.argsort(flat_e)
    sorted_e = flat_e[order]
    sorted_tok = (order // TOP_K).astype(jnp.int32)
    counts = jnp.bincount(flat_e, length=N_EXPERTS).astype(jnp.int32)
    padded = (counts + MOE_BLOCK - 1) // MOE_BLOCK * MOE_BLOCK
    pad_end = jnp.cumsum(padded)
    pad_start = pad_end - padded
    start = jnp.cumsum(counts) - counts
    dest = pad_start[sorted_e] + (jnp.arange(n_assign, dtype=jnp.int32) - start[sorted_e])
    cap = (-(-n_assign // MOE_BLOCK) + N_EXPERTS) * MOE_BLOCK
    n_blocks = cap // MOE_BLOCK
    slot_tok = jnp.full((cap,), T, dtype=jnp.int32).at[dest].set(sorted_tok)
    block_e = jnp.minimum(
        jnp.searchsorted(pad_end, jnp.arange(n_blocks, dtype=jnp.int32) * MOE_BLOCK, side='right'),
        N_EXPERTS - 1)
    h_pad = jnp.concatenate([h, jnp.zeros((1, D), h.dtype)], axis=0)

    def expert_block(args):
        tok, e = args
        xb = h_pad[tok]
        return (jax.nn.silu(xb @ w_gate[e]) * (xb @ w_up[e])) @ w_down[e]

    y_slots = lax.map(expert_block, (slot_tok.reshape(n_blocks, MOE_BLOCK), block_e))
    y_assign = y_slots.reshape(cap, D)[dest]
    w_assign = gates.reshape(-1)[order]
    return jnp.zeros((T, D), h.dtype).at[sorted_tok].add(y_assign * w_assign[:, None])

def trunk(x, past_a, past_c, past_d, start_pos, p):
    bsz, L, _ = x.shape
    h = layer_norm(x, p['ln_in_g'], p['ln_in_b'])
    end_pos = start_pos + L
    n_cur = end_pos - ((end_pos - 1) // CHUNK) * CHUNK
    outs_a, outs_c, outs_d, outs_v = [], [], [], []
    for i in range(DEPTH):
        z = h @ p['w_in'][i]
        a_val, a_gate, b_u, b_v, c_x, c_b, c_c, d_in = jnp.split(z, SPLIT_POINTS, axis=-1)
        a_glu = a_val * jax.nn.sigmoid(a_gate)
        a_conv, buf_a = causal_depthwise_conv(past_a[i], a_glu, p['conv_a_w'][i])
        y_a = jax.nn.silu(layer_norm(a_conv + p['conv_a_b'][i], p['ln_a_g'][i], p['ln_a_b'][i]))
        u = jax.nn.gelu(b_u, approximate=False)
        v = layer_norm(jax.nn.gelu(b_v, approximate=False), p['ln_v_g'][i], p['ln_v_b'][i])
        y_b = chunk_gmlp(u, v, p['w_s'][i], p['b_s'][i])
        c_conv, buf_c = causal_depthwise_conv(past_c[i], c_c * c_x, p['conv_c_w'][i])
        y_c = c_b * c_conv
        y_d, buf_d = pool_mixer(past_d[i], d_in, p['w_pool'][i], p['pool_scale'][i], start_pos)
        mix = jnp.concatenate([y_a, y_b, y_c, y_d], axis=-1) @ p['w_out'][i]
        h = layer_norm(ALPHA * h + mix, p['ln_mix_g'][i], p['ln_mix_b'][i])
        flat = h.reshape(bsz * L, D_MODEL)
        j = i // 2
        if i % 2 == 0:
            f = dense_swiglu(flat, p['w_ff_gate'][j], p['w_ff_up'][j], p['w_ff_down'][j])
        else:
            f = moe_swiglu(flat, p['w_router'][j], p['w_e_gate'][j], p['w_e_up'][j], p['w_e_down'][j])
        h = layer_norm(ALPHA * h + f.reshape(bsz, L, D_MODEL), p['ln_ffn_g'][i], p['ln_ffn_b'][i])
        outs_a.append(buf_a)
        outs_c.append(buf_c)
        outs_d.append(buf_d)
        outs_v.append(v[:, L - n_cur:])
    return h, jnp.stack(outs_a), jnp.stack(outs_c), jnp.stack(outs_d), jnp.stack(outs_v)

def setup_inputs(seed: int = 0) -> dict:
    key = jax.random.key(seed)
    ks = list(jax.random.split(key, 40))

    def nrm(idx, shape, scale):
        return jax.random.normal(ks[idx], shape, jnp.float32) * scale

    return {
        'x_prompt': nrm(0, (BATCH, SEQ, D_MODEL), 1.0),
        'x_sample': nrm(1, (DEC_BATCH, DEC_SEQ, D_MODEL), 1.0),
        'state_conv_a': nrm(2, (DEPTH, DEC_BATCH, CONV_A_W - 1, D_A), 0.5),
        'state_conv_c': nrm(3, (DEPTH, DEC_BATCH, CONV_C_W - 1, D_C), 1.0),
        'state_pool_d': nrm(4, (DEPTH, DEC_BATCH, POOL_PAST, D_D), 1.0),
        'ln_in_g': 1.0 + nrm(5, (D_MODEL,), 0.05),
        'ln_in_b': nrm(6, (D_MODEL,), 0.02),
        'w_in': nrm(7, (DEPTH, D_MODEL, D_IN), D_MODEL ** -0.5),
        'conv_a_w': nrm(8, (DEPTH, CONV_A_W, D_A), CONV_A_W ** -0.5),
        'conv_a_b': nrm(9, (DEPTH, D_A), 0.02),
        'ln_a_g': 1.0 + nrm(10, (DEPTH, D_A), 0.05),
        'ln_a_b': nrm(11, (DEPTH, D_A), 0.02),
        'ln_v_g': 1.0 + nrm(12, (DEPTH, D_B), 0.05),
        'ln_v_b': nrm(13, (DEPTH, D_B), 0.02),
        'w_s': nrm(14, (DEPTH, N_HEADS_B, CHUNK, CHUNK), CHUNK ** -0.5),
        'b_s': 1.0 + nrm(15, (DEPTH, N_HEADS_B, CHUNK), 0.05),
        'conv_c_w': nrm(16, (DEPTH, CONV_C_W, D_C), CONV_C_W ** -0.5),
        'w_pool': nrm(17, (DEPTH, N_POOL_GROUPS, POOL_GC, POOL_GC), POOL_GC ** -0.5),
        'pool_scale': 1.0 + nrm(18, (DEPTH, D_D), 0.05),
        'w_out': nrm(19, (DEPTH, D_MIX, D_MODEL), BETA * D_MIX ** -0.5),
        'ln_mix_g': 1.0 + nrm(20, (DEPTH, D_MODEL), 0.05),
        'ln_mix_b': nrm(21, (DEPTH, D_MODEL), 0.02),
        'w_ff_gate': nrm(22, (N_DENSE, D_MODEL, D_FF), D_MODEL ** -0.5),
        'w_ff_up': nrm(23, (N_DENSE, D_MODEL, D_FF), D_MODEL ** -0.5),
        'w_ff_down': nrm(24, (N_DENSE, D_FF, D_MODEL), BETA * D_FF ** -0.5),
        'w_router': nrm(25, (N_MOE, D_MODEL, N_EXPERTS), D_MODEL ** -0.5),
        'w_e_gate': nrm(26, (N_MOE, N_EXPERTS, D_MODEL, D_FF), D_MODEL ** -0.5),
        'w_e_up': nrm(27, (N_MOE, N_EXPERTS, D_MODEL, D_FF), D_MODEL ** -0.5),
        'w_e_down': nrm(28, (N_MOE, N_EXPERTS, D_FF, D_MODEL), BETA * D_FF ** -0.5),
        'ln_ffn_g': 1.0 + nrm(29, (DEPTH, D_MODEL), 0.05),
        'ln_ffn_b': nrm(30, (DEPTH, D_MODEL), 0.02),
    }

def reference(x_prompt, x_sample, state_conv_a, state_conv_c, state_pool_d,
              ln_in_g, ln_in_b, w_in, conv_a_w, conv_a_b, ln_a_g, ln_a_b, ln_v_g, ln_v_b,
              w_s, b_s, conv_c_w, w_pool, pool_scale, w_out, ln_mix_g, ln_mix_b,
              w_ff_gate, w_ff_up, w_ff_down, w_router, w_e_gate, w_e_up, w_e_down,
              ln_ffn_g, ln_ffn_b):
    p = dict(ln_in_g=ln_in_g, ln_in_b=ln_in_b, w_in=w_in, conv_a_w=conv_a_w, conv_a_b=conv_a_b,
             ln_a_g=ln_a_g, ln_a_b=ln_a_b, ln_v_g=ln_v_g, ln_v_b=ln_v_b, w_s=w_s, b_s=b_s,
             conv_c_w=conv_c_w, w_pool=w_pool, pool_scale=pool_scale, w_out=w_out,
             ln_mix_g=ln_mix_g, ln_mix_b=ln_mix_b, w_ff_gate=w_ff_gate, w_ff_up=w_ff_up,
             w_ff_down=w_ff_down, w_router=w_router, w_e_gate=w_e_gate, w_e_up=w_e_up,
             w_e_down=w_e_down, ln_ffn_g=ln_ffn_g, ln_ffn_b=ln_ffn_b)
    bsz = x_prompt.shape[0]
    dt = x_prompt.dtype
    zero_a = jnp.zeros((DEPTH, bsz, CONV_A_W - 1, D_A), dt)
    zero_c = jnp.zeros((DEPTH, bsz, CONV_C_W - 1, D_C), dt)
    zero_d = jnp.zeros((DEPTH, bsz, POOL_PAST, D_D), dt)
    y_prompt, conv_a_prompt, conv_c_prompt, pool_d_prompt, chunk_v_prompt = trunk(
        x_prompt, zero_a, zero_c, zero_d, 0, p)
    y_sample, conv_a_sample, conv_c_sample, pool_d_sample, chunk_v_sample = trunk(
        x_sample, state_conv_a, state_conv_c, state_pool_d, PAST_LEN, p)
    return (y_prompt, y_sample, conv_a_prompt, conv_c_prompt, pool_d_prompt, chunk_v_prompt,
            conv_a_sample, conv_c_sample, pool_d_sample, chunk_v_sample)


_drawn_inputs = setup_inputs


def setup_inputs(seed=0):
    import zlib

    import numpy as np

    out = dict(_drawn_inputs(seed))
    spreads = {}
    factors = {'conv_a_b': 3.331,
     'ln_a_g': 3.493,
     'ln_a_b': 15.333,
     'ln_v_b': 2.868,
     'b_s': 3.555,
     'pool_scale': 3.773}
    for name, (base, spread) in spreads.items():
        noise = np.random.default_rng([zlib.crc32(name.encode()), seed]).standard_normal(out[name].shape)
        drawn = base * np.exp(spread * noise) if base else spread * noise
        out[name] = __import__('jax').numpy.asarray(drawn.astype(out[name].dtype))
    for name, factor in factors.items():
        out[name] = (out[name] * factor).astype(out[name].dtype)
    return out
```

```python
from contextlib import ExitStack

import numpy as np

import concourse.bass as bass
from concourse import mybir

ALU = mybir.AluOpType
ACT = mybir.ActivationFunctionType
AX_X = mybir.AxisListType.X
F32 = mybir.dt.float32
I32 = mybir.dt.int32

P = 128
DEPTH, D_MODEL, SEQ, DEC_BATCH, DEC_SEQ = 2, 1024, 256, 8, 4
N_SAMPLE = DEC_BATCH * DEC_SEQ
TOKENS = SEQ + N_SAMPLE
KB = D_MODEL // P
MB = 2
TAPS_A, TAPS_C, POOL_PAST = 31, 3, 15
PAST_A, PAST_C = TAPS_A - 1, TAPS_C - 1
HEADS, CHUNK = 4, 128
D_FF, N_EXPERTS = 3584, 8
FB = D_FF // P
ALPHA = (2.0 * DEPTH) ** 0.25
LN_EPS = 1e-5
TT = 3
TILE_ROWS = [P, P, TOKENS - 2 * P]

SLOTS = 7
FPC = 4
CH = KB * FPC * P
GROUPS = FB // FPC
CPI = 3 * GROUPS
assert CPI % SLOTS == 0

W = 104
MAX_EXTRA = 2 * TOKENS // (W + 1)
LEVELS = (TOKENS - 1) // W
CAND = LEVELS * N_EXPERTS
N_ITEMS = N_EXPERTS + MAX_EXTRA + 1

LEN_A = PAST_A + SEQ + DEC_BATCH * (PAST_A + DEC_SEQ)
LEN_C = PAST_C + SEQ + DEC_BATCH * (PAST_C + DEC_SEQ)
LEN_D = POOL_PAST + SEQ + DEC_BATCH * (POOL_PAST + DEC_SEQ)

VEC = [("conv_a_w", TAPS_A * MB), ("conv_a_b", MB), ("ln_a_g", MB), ("ln_a_b", MB), ("ln_v_g", MB),
       ("ln_v_b", MB), ("conv_c_w", TAPS_C * MB), ("pool_scale", MB), ("ln_mix_g", KB),
       ("ln_mix_b", KB), ("ln_ffn_g", KB), ("ln_ffn_b", KB)]
VEC_LAYER = sum(n for _, n in VEC)
VEC_ALL = 2 * KB + DEPTH * VEC_LAYER

CST = [("ident", P), ("before", P), ("inv_count", MB * TOKENS), ("slot", W), ("rank8", N_EXPERTS),
       ("valid", TT), ("extra_no", MAX_EXTRA), ("earlier", CAND * CAND), ("cand_expert", CAND),
       ("cand_level", CAND)]
CST_ALL = sum(n for _, n in CST)

Z_BLOCKS = [2, 3, 0, 1, 6, 7, 4, 5, 14, 15, 12, 13, 8, 9, 10, 11]
Z_CHUNKS = [0, 1, 3, 2]
Z_BY_ACT = [0, 1, 4, 5, 6, 7, 8, 9, 10, 11]
Z_BY_DVE = [2, 3, 12, 13, 14, 15]
LNS = ["in", "v0", "a0", "mix0", "ffn0", "v1", "a1", "mix1", "ffn1"]
LN_BLOCKS = {n: (MB if n[0] in "va" else KB) for n in LNS}
LN_AT = {n: sum(LN_BLOCKS[m] for m in LNS[:i]) for i, n in enumerate(LNS)}


def vec_at(name, layer=None):
    if layer is None:
        return {"ln_in_g": 0, "ln_in_b": KB}[name]
    at = 2 * KB + layer * VEC_LAYER
    for n, size in VEC:
        if n == name:
            return at
        at += size
    raise KeyError(name)


def cst_at(name):
    at = 0
    for n, size in CST:
        if n == name:
            return at, size
        at += size
    raise KeyError(name)


def build(nc, t_in, t_out):
    ctx = ExitStack()
    with ctx:
        def sb(name, shape, dt=F32):
            return ctx.enter_context(nc.sbuf_tensor(name, shape, dt))

        def sem(name):
            return ctx.enter_context(nc.semaphore(name))

        ring = [sb(f"ring{i}", [P, CH]) for i in range(SLOTS)]
        h = sb("h", [P, KB, TOKENS])
        r = sb("r", [P, KB, TOKENS])
        ybuf = sb("ybuf", [P, KB * TOKENS])
        ext_a = sb("ext_a", [P, MB, LEN_A])
        ext_c = sb("ext_c", [P, MB, LEN_C])
        ext_d = sb("ext_d", [P, MB, LEN_D])
        work = sb("work", [P, FB * TOKENS])
        vec = sb("vec", [P, VEC_ALL])
        cst = sb("cst", [P, CST_ALL])
        ones = sb("ones", [P, P])
        ones_mix = sb("ones_mix", [P, P])
        ones_model = sb("ones_model", [P, P])
        ws_t = sb("ws_t", [P, DEPTH, HEADS, CHUNK])
        ws_s = sb("ws_s", [N_SAMPLE, DEPTH, HEADS, N_SAMPLE])
        bs = sb("bs", [P, DEPTH, MB, TOKENS])
        w_pool = sb("w_pool", [P, DEPTH, MB, P])
        w_router = sb("w_router", [P, KB, N_EXPERTS])
        diag = sb("diag", [P, TT, P])
        var_tok = sb("var_tok", [P, TT])
        rstd_tok = sb("rstd_tok", [P, TT])
        minus_half = sb("minus_half", [P, TT])
        table = sb("table", [1, 1 + MAX_EXTRA], I32)
        bank = [ctx.enter_context(nc.psum_tensor(f"bank{i}", [P, 512], F32)) for i in range(8)]

        def part(buf, at, *dims):
            n = int(np.prod(dims))
            v = buf[:, at:at + n]
            if len(dims) == 2:
                v = v.rearrange("p (a b) -> p a b", a=dims[0])
            if len(dims) == 3:
                v = v.rearrange("p (a b c) -> p a b c", a=dims[0], b=dims[1])
            return v, at + n

        at = 0
        acc_a, at = part(work, at, MB, TOKENS)
        sig, at = part(work, at, MB, TOKENS)
        gv, at = part(work, at, MB, TOKENS)
        vn, at = part(work, at, MB, TOKENS)
        gu, at = part(work, at, MB, TOKENS)
        cc, at = part(work, at, MB, TOKENS)
        sq_s, at = part(work, at, MB, TOKENS)
        acc_c, at = part(work, at, MB, LEN_C)
        sum_a, at = part(work, at, MB, LEN_D)
        sum_b, at = part(work, at, MB, LEN_D)
        v_tok, at = part(work, at, TT, MB * P)
        assert at <= FB * TOKENS
        dd = sig
        y = ybuf[:, :].rearrange("p (k t) -> p k t", k=KB)
        sq_l = y
        act_d = work[:, :].rearrange("p (f t) -> p f t", f=FB)
        gate_d, _ = part(ybuf, 0, 2, TOKENS)
        at = 0
        h_tok, at = part(work, at, TT, D_MODEL)
        xg, at = part(work, at, KB, W)
        gate_e, at = part(work, at, 2, FPC * W)
        act_e, at = part(work, at, 2, FPC * W)
        y_item, at = part(work, at, KB, W)
        sel, at = part(work, at, TT, W)
        sel_w, at = part(work, at, TT, W)
        at = 0
        y_tok, at = part(ybuf, at, D_MODEL)
        scat, at = part(ybuf, at, TOKENS)
        item_pos, at = part(ybuf, at, TT, N_ITEMS)
        item_gate, at = part(ybuf, at, TT, N_ITEMS)
        logit, at = part(ybuf, at, TT, N_EXPERTS)
        key, at = part(ybuf, at, TT, N_EXPERTS)
        hot1, at = part(ybuf, at, TT, N_EXPERTS)
        hot2, at = part(ybuf, at, TT, N_EXPERTS)
        chosen, at = part(ybuf, at, TT, N_EXPERTS)
        cand_pos, at = part(ybuf, at, TT, CAND)
        cand_gate, at = part(ybuf, at, TT, CAND)
        col, at = part(ybuf, at, 8, TT)
        counts, at = part(ybuf, at, N_EXPERTS)
        is_extra, at = part(ybuf, at, CAND)
        extra_rank, at = part(ybuf, at, CAND)
        picked, at = part(ybuf, at, MAX_EXTRA, CAND)
        tmp, at = part(ybuf, at, max(MAX_EXTRA, CAND) * CAND)
        tab_f, at = part(ybuf, at, 1 + MAX_EXTRA)
        assert at <= KB * TOKENS

        def const(name, dims=None):
            a, n = cst_at(name)
            v = cst[:, a:a + n]
            return v.rearrange("p (a b) -> p a b", a=dims) if dims else v

        ident = const("ident")
        before = const("before")

        ring_in = [sem(f"ring_in{i}") for i in range(SLOTS)]
        x_in, vec_in, cst_in, par_in = sem("x_in"), sem("vec_in"), sem("cst_in"), sem("par_in")
        past_a, past_c, past_d = sem("past_a"), sem("past_c"), sem("past_d")
        ones_ready, setup = sem("ones_ready"), sem("setup")
        pool_set = sem("pool_set")
        ln_mean, ln_xc, ln_sq, ln_var = sem("ln_mean"), sem("ln_xc"), sem("ln_sq"), sem("ln_var")
        ln_ve, ln_rs, ln_xn, ln_out = sem("ln_ve"), sem("ln_rs"), sem("ln_xn"), sem("ln_out")
        ln_spread = sem("ln_spread")
        z_ready, z_act, z_dve = sem("z_ready"), sem("z_act"), sem("z_dve")
        conv_a, conv_c, gated_c = sem("conv_a"), sem("conv_c"), sem("gated_c")
        v_turned, v_tok_dve, v_tok_act = sem("v_turned"), sem("v_tok_dve"), sem("v_tok_act")
        mixed_b, b_sum, y_b = sem("mixed_b"), sem("b_sum"), sem("y_b")
        pool_step, mapped_d, y_d = sem("pool_step"), sem("mapped_d"), sem("y_d")
        proj_ready, r_ready = sem("proj_ready"), sem("r_ready")
        gate_ready, up_ready, silu_done, act_done = (sem("gate_ready"), sem("up_ready"),
                                                     sem("silu_done"), sem("act_done"))
        down_chunk = sem("down_chunk")
        st_a, st_c, st_d, st_v, st_y = sem("st_a"), sem("st_c"), sem("st_d"), sem("st_v"), sem("st_y")
        logits_ready, h_turned, h_tok_dve, h_tok_act = (sem("logits_ready"), sem("h_turned"),
                                                        sem("h_tok_dve"), sem("h_tok_act"))
        route, exp_done, chosen_ready, pos_ready = (sem("route"), sem("exp_done"),
                                                    sem("chosen_ready"), sem("pos_ready"))
        table_ready, chosen_top = sem("table_ready"), sem("chosen_top")
        chunk_done = sem("chunk_done")
        sel_ready, sel_w_ready, gathered = sem("sel_ready"), sem("sel_w_ready"), sem("gathered")
        xg_dve, xg_act = sem("xg_dve"), sem("xg_act")
        sel_turned, scat_ready = sem("sel_turned"), sem("scat_ready")
        e_silu, e_act = sem("e_silu"), sem("e_act")
        yi_dve, yi_act, y_turned = sem("yi_dve"), sem("yi_act"), sem("y_turned")
        yt_dve, yt_act, scattered, added = (sem("yt_dve"), sem("yt_act"), sem("scattered"),
                                            sem("added"))

        def prompt_of(ext, b, past):
            return ext[:, b, past:past + SEQ]

        def samples_of(ext, b, past, lo, hi):
            return ext[:, b, past + SEQ:].rearrange("p (s l) -> p s l", s=DEC_BATCH)[:, :, lo:hi]

        def sample_cols(v):
            return v[:, SEQ:TOKENS].rearrange("p (s l) -> p s l", s=DEC_BATCH)

        def in_chunk(w, c):
            return w[:, c * FPC * P:(c + 1) * FPC * P].rearrange("(k p) n -> p k n", p=P)

        def down_rows(w, c):
            return w[c * FPC * P:(c + 1) * FPC * P, :].rearrange("(k p) n -> p k n", p=P)

        stream = []
        proj_uses = 0
        for layer in range(DEPTH):
            for j, c in enumerate(Z_CHUNKS):
                stream.append((in_chunk(t_in["w_in"][layer], c), z_ready, 16 * layer + 4 * (j + 1)))
            for j in range(2):
                stream.append((in_chunk(t_in["w_out"][layer], j), proj_ready, 8 * proj_uses + 4 * (j + 1)))
            proj_uses += 1
            if layer == 0:
                for g in range(GROUPS):
                    stream.append((in_chunk(t_in["w_ff_gate"][0], g), gate_ready, FPC * (g + 1)))
                    stream.append((in_chunk(t_in["w_ff_up"][0], g), up_ready, FPC * (g + 1)))
                for g in range(GROUPS):
                    done = (down_chunk, g + 1) if g < GROUPS - 1 else (proj_ready, 8 * proj_uses + 8)
                    stream.append((down_rows(t_in["w_ff_down"][0], g), *done))
                proj_uses += 1
        START = len(stream)
        item_chunks = [("gate", 0), ("up", 0)]
        for g in range(1, GROUPS):
            item_chunks += [("gate", g), ("up", g), ("down", g - 1)]
        item_chunks.append(("down", GROUPS - 1))
        item_place = {c: p for p, c in enumerate(item_chunks)}

        def arrived(eng, c):
            eng.wait_ge(ring_in[c % SLOTS], 16 * (c // SLOTS + 1))

        def item_arrived(eng, i, p):
            c = START + p
            eng.wait_ge(ring_in[c % SLOTS], i * (16 * CPI // SLOTS) + 16 * (c // SLOTS + 1))

        def slot_of(c):
            return ring[c % SLOTS][:, :].rearrange("p (k n) -> p k n", n=FPC * P)

        def down_of(c):
            return ring[c % SLOTS][:, :].rearrange("p (k n) -> p k n", n=D_MODEL)

        block = ctx.enter_context(nc.Block())

        @block.sync
        def _(sp):
            xt = t_in["x_t"].rearrange("(k p) t -> p k t", p=P)
            for half in range(2):
                sp.dma_start(h[:, 4 * half:4 * half + 4, :], xt[:, 4 * half:4 * half + 4, :]).then_inc(x_in, 16)
            for c, (src, _, _) in enumerate(stream):
                if c >= SLOTS:
                    sp.wait_ge(stream[c - SLOTS][1], stream[c - SLOTS][2])
                slot = down_of(c) if src.shape[2] == D_MODEL else slot_of(c)
                sp.dma_start(slot, src).then_inc(ring_in[c % SLOTS], 16)

            names = {"gate": "w_e_gate", "up": "w_e_up", "down": "w_e_down"}

            def load_item(i, expert, first):
                for p, (kind, g) in enumerate(item_chunks):
                    c = START + p
                    if first and p < SLOTS:
                        sp.wait_ge(stream[c - SLOTS][1], stream[c - SLOTS][2])
                    else:
                        sp.wait_ge(chunk_done, i * CPI + (p - SLOTS + 1))
                    w = t_in[names[kind]][0]
                    if kind == "down":
                        src = w[bass.ds(expert, 1), g * FPC * P:(g + 1) * FPC * P, :]
                        slot = down_of(c)
                    else:
                        src = w[bass.ds(expert, 1), :, g * FPC * P:(g + 1) * FPC * P]
                        slot = slot_of(c)
                    src = src.rearrange("e (k p) n -> p (e k) n", p=P)
                    sp.dma_start(slot, src).then_inc(ring_in[c % SLOTS], 16)

            load_item(0, 0, True)
            with sp.Fori(1, N_EXPERTS) as i:
                load_item(i, i, False)
            sp.wait_ge(table_ready, 1)
            n_items = sp.value_load(table[0:1, 0:1], min_val=N_EXPERTS, max_val=N_EXPERTS + MAX_EXTRA)
            with sp.If(n_items > N_EXPERTS):
                with sp.Fori(N_EXPERTS, n_items) as i:
                    expert = sp.value_load(table[0:1, bass.ds(i - (N_EXPERTS - 1), 1)],
                                           min_val=0, max_val=N_EXPERTS - 1)
                    load_item(i, expert, False)
            y_out = t_out["y_t"].rearrange("(k p) t -> p k t", p=P)
            for half in range(2):
                sp.wait_ge(ln_out, LN_AT["ffn1"] + 4 * (half + 1))
                sp.dma_start(y_out[:, 4 * half:4 * half + 4, :], h[:, 4 * half:4 * half + 4, :]).then_inc(st_y, 16)
            sp.wait_ge(st_y, 32)

        @block.tensor
        def _(pe):
            mm = nc.tensor.matmul

            def ln_sums(name, x, sq, weights, ready):
                n, nb = LNS.index(name), LN_BLOCKS[name]
                for b in range(nb):
                    ready(b)
                    last = mm(bank[6][:, 0:TOKENS], weights[:, :], x[:, b, :], start=(b == 0), stop=(b == nb - 1))
                last.then_inc(ln_mean, 1)
                yield
                for b in range(nb):
                    pe.wait_ge(ln_sq, LN_AT[name] + b + 1)
                    last = mm(bank[7][:, 0:TOKENS], weights[:, :], sq[:, b, :], start=(b == 0), stop=(b == nb - 1))
                last.then_inc(ln_var, 1)
                yield
                pe.wait_ge(ln_rs, n + 1)
                for t in range(TT):
                    rows = TILE_ROWS[t]
                    last = mm(bank[7][:, t * P:t * P + rows], rstd_tok[0:rows, t:t + 1].broadcast_to([rows, P]),
                              ident[0:rows, 0:rows], start=True, stop=True)
                last.then_inc(ln_spread, 1)
                yield

            def large_ln(name, ready):
                for _ in ln_sums(name, r if name != "in" else h, sq_l, ones_model, ready):
                    pass

            def z_block(layer, n, c0):
                if n % 4 == 0:
                    arrived(pe, c0 + n // 4)
                if n >= 6:
                    if n - 6 in Z_BY_ACT:
                        pe.wait_ge(z_act, len(Z_BY_ACT) * layer + Z_BY_ACT.index(n - 6) + 1)
                    else:
                        pe.wait_ge(z_dve, len(Z_BY_DVE) * layer + Z_BY_DVE.index(n - 6) + 1)
                at = Z_BLOCKS[n] % FPC * P
                for k in range(KB):
                    last = mm(bank[n % 6][:, 0:TOKENS], slot_of(c0 + n // 4)[:, k, at:at + P], h[:, k, :],
                              start=(k == 0), stop=(k == KB - 1))
                last.then_inc(z_ready, 1)

            def mixer(layer, c0):
                ln_in = "in" if layer == 0 else "ffn0"
                name_v, name_a = f"v{layer}", f"a{layer}"
                pe.wait_ge(ln_out, LN_AT[ln_in] + KB)
                ln_v = ln_sums(name_v, gv, sq_s, ones_mix,
                               lambda b: pe.wait_ge(z_act, 10 * layer + 3 + b))
                ln_a = ln_sums(name_a, acc_a, sq_s, ones_mix,
                               lambda b: pe.wait_ge(conv_a, 4 * TAPS_A * (layer + 1)))
                for n in range(10):
                    z_block(layer, n, c0)
                next(ln_v)
                for n in range(10, 12):
                    z_block(layer, n, c0)
                next(ln_v)
                z_block(layer, 12, c0)
                next(ln_v)
                pe.wait_ge(ln_xc, LN_AT[name_v] + MB)
                next(ln_a)
                for n in range(13, 15):
                    z_block(layer, n, c0)
                pe.wait_ge(ln_xn, LN_AT[name_v] + MB)
                next(ln_a)
                z_block(layer, 15, c0)
                next(ln_a)
                for b in range(MB):
                    pe.wait_ge(pool_step, 8 * (layer + 1))
                    pe.wait_ge(z_act, 10 * (layer + 1))
                    mm(bank[4 + b][:, 0:TOKENS], w_pool[:, layer, b, :], dd[:, b, :],
                       start=True, stop=True).then_inc(mapped_d, 1)
                pe.wait_ge(ln_out, LN_AT[name_v] + MB)
                pe.wait_ge(ln_xc, LN_AT[name_a] + MB)
                for t in range(2):
                    for b in range(MB):
                        last = nc.tensor.transpose(bank[6][:, t * 256 + b * P:t * 256 + (b + 1) * P],
                                                   vn[:, b, t * P:(t + 1) * P], ident)
                last.then_inc(v_turned, 1)
                pe.wait_ge(ln_xn, LN_AT[name_a] + MB)
                for b in range(MB):
                    last = nc.tensor.transpose(bank[7][0:N_SAMPLE, b * P:(b + 1) * P], vn[:, b, SEQ:TOKENS], ident)
                last.then_inc(v_turned, 1)
                pe.wait_ge(v_tok_dve, layer + 1)
                pe.wait_ge(v_tok_act, layer + 1)
                pe.wait_ge(z_dve, len(Z_BY_DVE) * layer + 4)
                for b in range(MB):
                    for half in range(2):
                        head, lo = 2 * b + half, 64 * half
                        for t in range(2):
                            mm(bank[b][lo:lo + 64, t * P:(t + 1) * P], v_tok[:, t, head * 64:head * 64 + 64],
                               ws_t[:, layer, head, :], start=True, stop=True)
                        last = mm(bank[b][lo:lo + 64, SEQ:TOKENS], v_tok[0:N_SAMPLE, 2, head * 64:head * 64 + 64],
                                  ws_s[:, layer, head, :], start=True, stop=True)
                    last.then_inc(mixed_b, 1)
                c1 = c0 + len(Z_CHUNKS)
                for d in range(KB):
                    if d % FPC == 0:
                        arrived(pe, c1 + d // FPC)
                    at = d % FPC * P
                    for j, k in enumerate([6, 7, 4, 5, 0, 1, 2, 3]):
                        if d == 0 and k == 6:
                            pe.wait_ge(y_d, 2 * (layer + 1))
                        if d == 0 and k == 4:
                            pe.wait_ge(z_dve, len(Z_BY_DVE) * (layer + 1))
                        if d == 0 and k == 0:
                            pe.wait_ge(ln_out, LN_AT[name_a] + MB)
                        if d == 0 and k == 2:
                            pe.wait_ge(y_b, 2 * (layer + 1))
                        last = mm(bank[(6 + d) % 8][:, 0:TOKENS], slot_of(c1 + d // FPC)[:, k, at:at + P], y[:, k, :],
                                  start=(j == 0), stop=(j == KB - 1))
                    last.then_inc(proj_ready, 1)
                return c1 + 2

            def dense(c0):
                pe.wait_ge(ln_out, LN_AT["mix0"] + KB)
                for f in range(FB):
                    g = f // FPC
                    if f % FPC == 0:
                        arrived(pe, c0 + 2 * g)
                        arrived(pe, c0 + 2 * g + 1)
                    if f >= 3:
                        pe.wait_ge(act_done, f - 2)
                    at = f % FPC * P
                    for which, ready in ((0, gate_ready), (1, up_ready)):
                        for k in range(KB):
                            last = mm(bank[2 * (f % 3) + which][:, 0:TOKENS],
                                      slot_of(c0 + 2 * g + which)[:, k, at:at + P], h[:, k, :],
                                      start=(k == 0), stop=(k == KB - 1))
                        last.then_inc(ready, 1)
                c0 += 2 * GROUPS
                pe.wait_ge(act_done, FB)
                for f in range(FB):
                    g = f // FPC
                    if f % FPC == 0:
                        arrived(pe, c0 + g)
                    for d in range(KB):
                        last = mm(bank[(6 + d) % 8][:, 0:TOKENS], down_of(c0 + g)[:, f % FPC, d * P:(d + 1) * P],
                                  act_d[:, f, :], start=(f == 0), stop=(f == FB - 1), skip_group_check=True)
                        if f == FB - 1:
                            last.then_inc(proj_ready, 1)
                    if f % FPC == FPC - 1 and f < FB - 1:
                        last.then_inc(down_chunk, 1)
                return c0 + GROUPS

            pe.wait_ge(ones_ready, 1)
            pe.wait_ge(x_in, 32)
            pe.wait_ge(cst_in, 16)
            large_ln("in", lambda b: None)
            pe.wait_ge(setup, 1)
            pe.wait_ge(par_in, PARAMS * 16)
            pe.wait_ge(cst_in, 16)
            c = mixer(0, 0)
            large_ln("mix0", lambda b: pe.wait_ge(r_ready, b + 1))
            c = dense(c)
            large_ln("ffn0", lambda b: pe.wait_ge(r_ready, KB + b + 1))
            c = mixer(1, c)
            large_ln("mix1", lambda b: pe.wait_ge(r_ready, 2 * KB + b + 1))

            pe.wait_ge(ln_out, LN_AT["mix1"] + KB)
            for t in range(TT):
                rows = TILE_ROWS[t]
                for k in range(KB):
                    last = mm(bank[0][0:rows, t * 8:t * 8 + 8], h[:, k, t * P:t * P + rows], w_router[:, k, :],
                              start=(k == 0), stop=(k == KB - 1))
            last.then_inc(logits_ready, 1)
            for t in range(TT):
                rows = TILE_ROWS[t]
                for half in range(2):
                    for k in range(4):
                        last = nc.tensor.transpose(bank[2 + 2 * t + half][0:rows, k * P:(k + 1) * P],
                                                   h[:, 4 * half + k, t * P:t * P + rows], ident)
                    last.then_inc(h_turned, 1)
            pe.wait_ge(chosen_ready, 1)
            for t in range(TT):
                for s in range(t + 1):
                    mm(bank[1][:, t * 8:t * 8 + 8], (before if s == t else ones)[:, :], chosen[:, s, :],
                       start=(s == 0), stop=(s == t))
            for s in range(TT):
                last = mm(bank[1][:, 24:32], ones[:, :], chosen[:, s, :], start=(s == 0), stop=(s == TT - 1))
            last.then_inc(pos_ready, 1)

            def gather(n):
                pe.wait_ge(sel_ready, n + 1)
                for k in range(KB):
                    for t in range(TT):
                        rows = TILE_ROWS[t]
                        last = mm(bank[6 + k // 4][:, k % 4 * W:(k % 4 + 1) * W],
                                  h_tok[0:rows, t, k * P:(k + 1) * P], sel[0:rows, t, :],
                                  start=(t == 0), stop=(t == TT - 1))
                last.then_inc(gathered, 1)

            pe.wait_ge(h_tok_dve, 3)
            pe.wait_ge(h_tok_act, 3)
            gather(0)
            pe.wait_ge(table_ready, 1)
            n_items = pe.value_load(table[0:1, 0:1], min_val=N_EXPERTS, max_val=N_EXPERTS + MAX_EXTRA)
            with pe.Fori(0, n_items) as i:
                def hidden(g):
                    for which, kind in ((0, "gate"), (1, "up")):
                        p = item_place[kind, g]
                        item_arrived(pe, i, p)
                        if g >= 2 and which == 0:
                            pe.wait_ge(e_act, i * GROUPS + g - 1)
                        for f in range(FPC):
                            for k in range(KB):
                                last = mm(bank[2 * (g % 2) + which][:, f * W:(f + 1) * W],
                                          slot_of(START + p)[:, k, f * P:(f + 1) * P], xg[:, k, :],
                                          start=(k == 0), stop=(k == KB - 1))
                        last.then_inc(chunk_done, 1)

                def down(g):
                    p = item_place["down", g]
                    item_arrived(pe, i, p)
                    pe.wait_ge(e_act, i * GROUPS + g + 1)
                    for f in range(FPC):
                        for d in range(KB):
                            last = mm(bank[4 + d // 4][:, d % 4 * W:(d % 4 + 1) * W],
                                      down_of(START + p)[:, f, d * P:(d + 1) * P],
                                      act_e[:, g % 2, f * W:(f + 1) * W],
                                      start=(g == 0 and f == 0 and d % 4 == 0),
                                      stop=(g == GROUPS - 1 and f == FPC - 1), skip_group_check=True)
                    last.then_inc(chunk_done, 1)

                pe.wait_ge(xg_dve, i + 1)
                pe.wait_ge(xg_act, i + 1)
                pe.wait_ge(added, i * KB + KB)
                hidden(0)
                pe.wait_ge(sel_w_ready, i + 1)
                for t in range(TT):
                    rows = TILE_ROWS[t]
                    last = nc.tensor.transpose(bank[6][0:W, t * P:t * P + rows], sel_w[0:rows, t, :],
                                               ident[0:rows, 0:rows])
                last.then_inc(sel_turned, 1)
                for g in range(1, GROUPS):
                    hidden(g)
                    down(g - 1)
                down(GROUPS - 1)
                pe.wait_ge(scat_ready, i + 1)
                gather(i + 1)
                pe.wait_ge(yi_dve, i + 1)
                pe.wait_ge(yi_act, i + 1)
                for d in range(KB):
                    last = nc.tensor.transpose(bank[4 + d // 4][0:W, d % 4 * P:(d % 4 + 1) * P],
                                               y_item[:, d, :], ident)
                    if d % 4 == 3:
                        last.then_inc(y_turned, 1)
                for d in range(KB):
                    if d == 0:
                        pe.wait_ge(yt_dve, i + 1)
                    if d == 4:
                        pe.wait_ge(yt_act, i + 1)
                    if d >= 4:
                        pe.wait_ge(added, (i + 1) * KB + d - 3)
                    mm(bank[d % 4][:, 0:TOKENS], y_tok[0:W, d * P:(d + 1) * P], scat[0:W, :],
                       start=True, stop=True).then_inc(scattered, 1)
            pe.wait_ge(added, n_items * KB + KB)
            large_ln("ffn1", lambda b: None)

        @block.scalar
        def _(act):
            A = nc.scalar.activation

            def v_at(name, layer, b):
                a = vec_at(name, layer) + b
                return vec[:, a:a + 1]

            def ln_squares(name, x, sq):
                for b in range(LN_BLOCKS[name]):
                    act.wait_ge(ln_xc, LN_AT[name] + b + 1)
                    A(sq[:, b, :], x[:, b, :], ACT.Square).then_inc(ln_sq, 1)

            def ln_gain(name, x, out, g, bias, func=ACT.Identity):
                for b in range(LN_BLOCKS[name]):
                    act.wait_ge(ln_xn, LN_AT[name] + b + 1)
                    A(out[:, b, :], x[:, b, :], func, scale=vec[:, g + b:g + b + 1],
                      bias=vec[:, bias + b:bias + b + 1]).then_inc(ln_out, 1)

            def z_out(layer, n, func, *outs):
                act.wait_ge(z_ready, 16 * layer + n + 1)
                b = bank[n % 6]
                if len(outs) == 1:
                    last = A(outs[0], b[:, 0:TOKENS], func)
                else:
                    A(outs[0], b[:, 0:SEQ], func)
                    last = A(outs[1], sample_cols(b), func)
                last.then_inc(z_act, 1)

            def mixer(layer):
                for b in range(MB):
                    z_out(layer, b, ACT.Sigmoid, sig[:, b, :])
                for b in range(MB):
                    z_out(layer, 4 + b, ACT.Gelu, gv[:, b, :])
                for b in range(MB):
                    z_out(layer, 6 + b, ACT.Gelu, gu[:, b, :])
                if layer:
                    act.wait_ge(pool_step, 8)
                    act.wait_ge(st_d, 64)
                for b in range(MB):
                    z_out(layer, 8 + b, ACT.Copy, prompt_of(ext_d, b, POOL_PAST),
                          samples_of(ext_d, b, POOL_PAST, POOL_PAST, POOL_PAST + DEC_SEQ))
                for b in range(MB):
                    z_out(layer, 10 + b, ACT.Copy, cc[:, b, :])
                ln_squares(f"v{layer}", gv, sq_s)
                ln_gain(f"v{layer}", gv, vn, vec_at("ln_v_g", layer), vec_at("ln_v_b", layer))
                ln_squares(f"a{layer}", acc_a, sq_s)
                for b in range(MB):
                    act.wait_ge(mapped_d, 2 * layer + b + 1)
                    A(y[:, 6 + b, :], bank[4 + b][:, 0:TOKENS], ACT.Copy,
                      scale=v_at("pool_scale", layer, b)).then_inc(y_d, 1)
                ln_gain(f"a{layer}", acc_a, y, vec_at("ln_a_g", layer), vec_at("ln_a_b", layer), ACT.Silu)
                act.wait_ge(v_turned, 2 * layer + 2)
                A(v_tok[0:N_SAMPLE, 2, :], bank[7][0:N_SAMPLE, 0:MB * P], ACT.Copy).then_inc(v_tok_act, 1)

            def large_ln(name, g, bias):
                x = h if name == "in" else r
                ln_squares(name, x, sq_l)
                ln_gain(name, x, h, g, bias)

            act.wait_ge(vec_in, 16)
            large_ln("in", vec_at("ln_in_g"), vec_at("ln_in_b"))
            mixer(0)
            large_ln("mix0", vec_at("ln_mix_g", 0), vec_at("ln_mix_b", 0))
            for f in range(FB):
                act.wait_ge(gate_ready, f + 1)
                if f >= 2:
                    act.wait_ge(act_done, f - 1)
                A(gate_d[:, f % 2, :], bank[2 * (f % 3)][:, 0:TOKENS], ACT.Silu).then_inc(silu_done, 1)
            large_ln("ffn0", vec_at("ln_ffn_g", 0), vec_at("ln_ffn_b", 0))
            mixer(1)
            large_ln("mix1", vec_at("ln_mix_g", 1), vec_at("ln_mix_b", 1))

            act.wait_ge(st_v, 128)
            for t in range(TT):
                rows = TILE_ROWS[t]
                act.wait_ge(h_turned, 2 * t + 2)
                A(h_tok[0:rows, t, 512:1024], bank[3 + 2 * t][0:rows, :], ACT.Copy).then_inc(h_tok_act, 1)
            act.wait_ge(route, 5)
            A(col[:, 2, :], col[:, 2, :], ACT.Exp).then_inc(exp_done, 1)
            act.wait_ge(gathered, 1)
            A(xg[:, 4:8, :], bank[7][:, 0:4 * W].rearrange("p (k n) -> p k n", k=4), ACT.Copy).then_inc(xg_act, 1)
            act.wait_ge(table_ready, 1)
            n_items = act.value_load(table[0:1, 0:1], min_val=N_EXPERTS, max_val=N_EXPERTS + MAX_EXTRA)
            with act.Fori(0, n_items) as i:
                for g in range(GROUPS):
                    act.wait_ge(chunk_done, i * CPI + item_place["gate", g] + 1)
                    if g >= 2:
                        act.wait_ge(e_act, i * GROUPS + g - 1)
                    A(gate_e[:, g % 2, :], bank[2 * (g % 2)][:, 0:FPC * W], ACT.Silu).then_inc(e_silu, 1)
                    if g == 0:
                        act.wait_ge(sel_turned, i + 1)
                        A(scat[0:W, :], bank[6][0:W, 0:TOKENS], ACT.Copy).then_inc(scat_ready, 1)
                act.wait_ge(chunk_done, i * CPI + CPI)
                A(y_item[:, 4:8, :], bank[5][:, 0:4 * W].rearrange("p (k n) -> p k n", k=4),
                  ACT.Copy).then_inc(yi_act, 1)
                act.wait_ge(gathered, i + 2)
                A(xg[:, 4:8, :], bank[7][:, 0:4 * W].rearrange("p (k n) -> p k n", k=4),
                  ACT.Copy).then_inc(xg_act, 1)
                act.wait_ge(y_turned, i * 2 + 2)
                A(y_tok[0:W, 512:1024], bank[5][0:W, :], ACT.Copy).then_inc(yt_act, 1)
            large_ln("ffn1", vec_at("ln_ffn_g", 1), vec_at("ln_ffn_b", 1))

        @block.vector
        def _(dve):
            V = nc.vector

            def v_at(name, layer, b):
                a = vec_at(name, layer) + b
                return vec[:, a:a + 1]

            def ln_centre(name, x):
                dve.wait_ge(ln_mean, LNS.index(name) + 1)
                for b in range(LN_BLOCKS[name]):
                    V.tensor_tensor(x[:, b, :], x[:, b, :], bank[6][:, 0:TOKENS], ALU.subtract).then_inc(ln_xc, 1)

            def ln_scale(name, x):
                n = LNS.index(name)
                dve.wait_ge(ln_var, n + 1)
                for t in range(TT):
                    rows = TILE_ROWS[t]
                    last = V.tensor_tensor_reduce(out=diag[0:rows, t, 0:rows], in0=bank[7][0:rows, t * P:t * P + rows],
                                                  in1=ident[0:rows, 0:rows], scale=1.0, scalar=LN_EPS, op0=ALU.mult,
                                                  op1=ALU.add, accum_out=var_tok[0:rows, t:t + 1])
                last.then_inc(ln_ve, 1)
                dve.wait_ge(ln_spread, n + 1)
                for b in range(LN_BLOCKS[name]):
                    V.tensor_tensor(x[:, b, :], x[:, b, :], bank[7][:, 0:TOKENS], ALU.mult).then_inc(ln_xn, 1)

            def residual(use):
                for d in range(KB):
                    dve.wait_ge(proj_ready, KB * use + d + 1)
                    V.scalar_tensor_tensor(out=r[:, d, :], in0=h[:, d, :], scalar=ALPHA,
                                           in1=bank[(6 + d) % 8][:, 0:TOKENS], op0=ALU.mult,
                                           op1=ALU.add).then_inc(r_ready, 1)

            def mixer(layer):
                dve.wait_ge(past_a, 64 * (layer + 1))
                if layer:
                    dve.wait_ge(st_a, 64)
                for b in range(MB):
                    n = 2 + b
                    dve.wait_ge(z_ready, 16 * layer + n + 1)
                    dve.wait_ge(z_act, 10 * layer + b + 1)
                    V.tensor_tensor(prompt_of(ext_a, b, PAST_A), bank[n % 6][:, 0:SEQ], sig[:, b, 0:SEQ], ALU.mult)
                    V.tensor_tensor(samples_of(ext_a, b, PAST_A, PAST_A, PAST_A + DEC_SEQ),
                                    sample_cols(bank[n % 6]), sample_cols(sig[:, b, :]),
                                    ALU.mult).then_inc(z_dve, 1)
                dve.wait_ge(z_dve, 6 * layer + 2)
                steps = 4 * TAPS_A * layer
                for tap in range(TAPS_A):
                    for b in range(MB):
                        w = v_at("conv_a_w", layer, tap * MB + b)
                        for src, out in ((ext_a[:, b, tap:tap + SEQ], acc_a[:, b, 0:SEQ]),
                                         (samples_of(ext_a, b, PAST_A, tap, tap + DEC_SEQ), sample_cols(acc_a[:, b, :]))):
                            if tap == 0:
                                V.tensor_scalar(out, src, w, v_at("conv_a_b", layer, b), ALU.mult,
                                                ALU.add).then_inc(conv_a, 1)
                            else:
                                dve.wait_ge(conv_a, steps - 3)
                                V.scalar_tensor_tensor(out=out, in0=src, scalar=w, in1=out, op0=ALU.mult,
                                                       op1=ALU.add).then_inc(conv_a, 1)
                            steps += 1
                ln_centre(f"v{layer}", gv)
                ln_scale(f"v{layer}", gv)
                dve.wait_ge(past_c, 64 * (layer + 1))
                if layer:
                    dve.wait_ge(st_c, 64)
                for b in range(MB):
                    n = 12 + b
                    dve.wait_ge(z_ready, 16 * layer + n + 1)
                    dve.wait_ge(z_act, 10 * layer + 9 + b)
                    V.tensor_tensor(prompt_of(ext_c, b, PAST_C), bank[n % 6][:, 0:SEQ], cc[:, b, 0:SEQ], ALU.mult)
                    V.tensor_tensor(samples_of(ext_c, b, PAST_C, PAST_C, PAST_C + DEC_SEQ),
                                    sample_cols(bank[n % 6]), sample_cols(cc[:, b, :]),
                                    ALU.mult).then_inc(z_dve, 1)
                ln_centre(f"a{layer}", acc_a)
                n_out = LEN_C - PAST_C
                for tap in range(TAPS_C):
                    for b in range(MB):
                        w = v_at("conv_c_w", layer, tap * MB + b)
                        src, out = ext_c[:, b, tap:tap + n_out], acc_c[:, b, 0:n_out]
                        if tap == 0:
                            dve.wait_ge(z_dve, 6 * layer + 3 + b)
                            V.tensor_scalar(out, src, w, None, ALU.mult).then_inc(conv_c, 1)
                        else:
                            dve.wait_ge(conv_c, 6 * layer + 2 * (tap - 1) + b + 1)
                            V.scalar_tensor_tensor(out=out, in0=src, scalar=w, in1=out, op0=ALU.mult,
                                                   op1=ALU.add).then_inc(conv_c, 1)
                ln_scale(f"a{layer}", acc_a)
                for b in range(MB):
                    n = 14 + b
                    dve.wait_ge(z_ready, 16 * layer + n + 1)
                    dve.wait_ge(conv_c, 6 * layer + 5 + b)
                    V.tensor_tensor(y[:, 4 + b, 0:SEQ], bank[n % 6][:, 0:SEQ], acc_c[:, b, 0:SEQ], ALU.mult)
                    rows = acc_c[:, b, SEQ + PAST_C:LEN_C].rearrange("p (s l) -> p s l", s=DEC_BATCH)[:, :, 0:DEC_SEQ]
                    V.tensor_tensor(sample_cols(y[:, 4 + b, :]), sample_cols(bank[n % 6]), rows,
                                    ALU.mult).then_inc(z_dve, 1)
                dve.wait_ge(v_turned, 2 * layer + 1)
                V.tensor_copy(v_tok[:, 0:2, :], bank[6][:, :].rearrange("p (t n) -> p t n", t=2)).then_inc(v_tok_dve, 1)
                for b in range(MB):
                    dve.wait_ge(mixed_b, 2 * layer + b + 1)
                    V.tensor_tensor(cc[:, b, :], bank[b][:, 0:TOKENS], bs[:, layer, b, :], ALU.add).then_inc(b_sum, 1)
                    dve.wait_ge(b_sum, 2 * layer + b + 1)
                    V.tensor_tensor(y[:, 2 + b, :], cc[:, b, :], gu[:, b, :], ALU.mult).then_inc(y_b, 1)

            V.memset(ones_model[:, :], 1.0 / D_MODEL)
            V.memset(minus_half[:, :], -0.5)
            V.memset(var_tok[:, :], 1.0)
            V.memset(ones_mix[:, :], 1.0 / (MB * P))
            V.memset(ones[:, :], 1.0).then_inc(ones_ready, 1)
            V.memset(ext_a[:, :, 0:PAST_A], 0.0)
            V.memset(ext_c[:, :, 0:PAST_C], 0.0)
            V.memset(ext_d[:, :, 0:POOL_PAST], 0.0)
            V.memset(sum_a[:, :, 0:1], 0.0).then_inc(ones_ready, 1)
            ln_centre("in", h)
            dve.wait_ge(cst_in, 16)
            ln_scale("in", h)
            dve.wait_ge(par_in, PARAMS * 16)
            mixer(0)
            residual(0)
            ln_centre("mix0", r)
            ln_scale("mix0", r)
            dve.wait_ge(st_v, 64)
            for f in range(FB):
                dve.wait_ge(silu_done, f + 1)
                dve.wait_ge(up_ready, f + 1)
                V.tensor_tensor(act_d[:, f, :], gate_d[:, f % 2, :], bank[2 * (f % 3) + 1][:, 0:TOKENS],
                                ALU.mult).then_inc(act_done, 1)
            residual(1)
            ln_centre("ffn0", r)
            ln_scale("ffn0", r)
            mixer(1)
            residual(2)
            ln_centre("mix1", r)
            ln_scale("mix1", r)

            steps = [0]

            def step(ins):
                steps[0] += 1
                ins.then_inc(route, 1)
                dve.wait_ge(route, steps[0])

            def over_experts(v):
                return v.unsqueeze(2).broadcast_to([P, TT, N_EXPERTS])

            rank8 = const("rank8").unsqueeze(1).broadcast_to([P, TT, N_EXPERTS])
            dve.wait_ge(ln_out, LN_AT["mix1"] + KB)
            dve.wait_ge(st_v, 128)
            step(V.memset(logit[:, :, :], 0.0))
            dve.wait_ge(logits_ready, 1)
            V.tensor_copy(logit[:, 0:2, :], bank[0][:, 0:16].rearrange("p (t e) -> p t e", t=2))
            V.tensor_copy(logit[0:N_SAMPLE, 2, :], bank[0][0:N_SAMPLE, 16:24]).then_inc(route, 1)
            steps[0] += 1
            dve.wait_ge(route, steps[0])

            def top(values, hot, best):
                V.tensor_reduce(best, values, AX_X, ALU.max).then_inc(chosen_top, 1)
                tops[0] += 1
                dve.wait_ge(chosen_top, tops[0])
                for ins in (
                    lambda: V.tensor_tensor(key[:, :, :], values, over_experts(best), ALU.is_equal),
                    lambda: V.tensor_tensor(key[:, :, :], key[:, :, :], rank8, ALU.mult),
                    lambda: V.tensor_reduce(col[:, 7, :], key[:, :, :], AX_X, ALU.max),
                    lambda: V.tensor_tensor(hot, key[:, :, :], over_experts(col[:, 7, :]), ALU.is_equal),
                ):
                    ins().then_inc(chosen_top, 1)
                    tops[0] += 1
                    dve.wait_ge(chosen_top, tops[0])

            tops = [0]
            top(logit[:, :, :], hot1[:, :, :], col[:, 0, :])
            step(V.scalar_tensor_tensor(out=logit[:, :, :], in0=hot1[:, :, :], scalar=-3.0e38, in1=logit[:, :, :],
                                        op0=ALU.mult, op1=ALU.add))
            top(logit[:, :, :], hot2[:, :, :], col[:, 1, :])
            step(V.tensor_tensor(chosen[:, :, :], hot1[:, :, :], hot2[:, :, :], ALU.add))
            valid = over_experts(const("valid"))
            V.tensor_tensor(chosen[:, :, :], chosen[:, :, :], valid, ALU.mult).then_inc(chosen_ready, 1)
            for t in range(TT):
                dve.wait_ge(h_turned, 2 * t + 1)
                rows = TILE_ROWS[t]
                V.tensor_copy(h_tok[0:rows, t, 0:512], bank[2 + 2 * t][0:rows, :]).then_inc(h_tok_dve, 1)
            step(V.tensor_tensor(col[:, 2, :], col[:, 1, :], col[:, 0, :], ALU.subtract))
            dve.wait_ge(pos_ready, 1)
            dve.wait_ge(chosen_ready, 1)
            item_p = item_pos[:, :, 0:N_EXPERTS]
            step(V.scalar_tensor_tensor(out=item_p, in0=bank[1][:, 0:24].rearrange("p (t e) -> p t e", t=TT),
                                        scalar=1.0, in1=chosen[:, :, :], op0=ALU.add, op1=ALU.mult))
            step(V.tensor_scalar(item_p, item_p, -1.0, None, ALU.add))

            def select(dst, column, ready):
                for t in range(TT):
                    rows = TILE_ROWS[t]
                    last = V.tensor_scalar(dst[0:rows, t, :], const("slot")[0:rows, :], item_pos[0:rows, t, column],
                                           None, ALU.is_equal)
                last.then_inc(ready, 1)

            select(sel, slice(0, 1), sel_ready)
            dve.wait_ge(exp_done, 1)
            step(V.tensor_scalar(col[:, 3, :], col[:, 2, :], 1.0, None, ALU.add))
            step(V.reciprocal(col[:, 4, :], col[:, 3, :]))
            step(V.tensor_tensor(col[:, 5, :], col[:, 4, :], col[:, 2, :], ALU.mult))
            item_g = item_gate[:, :, 0:N_EXPERTS]
            step(V.tensor_tensor(item_g, hot1[:, :, :], over_experts(col[:, 4, :]), ALU.mult))
            step(V.tensor_tensor(hot2[:, :, :], hot2[:, :, :], over_experts(col[:, 5, :]), ALU.mult))
            step(V.tensor_tensor(item_g, item_g, hot2[:, :, :], ALU.add))
            step(V.tensor_copy(counts[:, :], bank[1][:, 24:32]))
            for m in range(LEVELS):
                a = m * N_EXPERTS
                V.tensor_scalar(is_extra[:, a:a + N_EXPERTS], counts[:, :], float((m + 1) * W), None, ALU.is_gt)
                V.tensor_scalar(cand_pos[:, :, a:a + N_EXPERTS], item_p, -float((m + 1) * W), None, ALU.add)
                step(V.tensor_copy(cand_gate[:, :, a:a + N_EXPERTS], item_g))
            square = tmp[:, 0:CAND * CAND].rearrange("p (a b) -> p a b", a=CAND)
            step(V.tensor_tensor(square, const("earlier", CAND),
                                 is_extra[:, :].unsqueeze(1).broadcast_to([P, CAND, CAND]), ALU.mult))
            step(V.tensor_reduce(extra_rank[:, :], square, AX_X, ALU.add))
            step(V.tensor_tensor(picked[:, :, :], extra_rank[:, :].unsqueeze(1).broadcast_to([P, MAX_EXTRA, CAND]),
                                 const("extra_no").unsqueeze(2).broadcast_to([P, MAX_EXTRA, CAND]), ALU.is_equal))
            step(V.tensor_tensor(picked[:, :, :], picked[:, :, :],
                                 is_extra[:, :].unsqueeze(1).broadcast_to([P, MAX_EXTRA, CAND]), ALU.mult))
            for src, dst in ((cand_pos, item_pos), (cand_gate, item_gate)):
                for t in range(TT):
                    prod = tmp[:, 0:MAX_EXTRA * CAND].rearrange("p (a b) -> p a b", a=MAX_EXTRA)
                    step(V.tensor_tensor(prod, picked[:, :, :],
                                         src[:, t, :].unsqueeze(1).broadcast_to([P, MAX_EXTRA, CAND]), ALU.mult))
                    step(V.tensor_reduce(dst[:, t, N_EXPERTS:N_EXPERTS + MAX_EXTRA], prod, AX_X, ALU.add))
                step(V.memset(dst[:, :, N_ITEMS - 1:N_ITEMS], 0.0))
            prod = tmp[:, 0:MAX_EXTRA * CAND].rearrange("p (a b) -> p a b", a=MAX_EXTRA)
            step(V.tensor_tensor(prod, picked[:, :, :],
                                 const("cand_expert").unsqueeze(1).broadcast_to([P, MAX_EXTRA, CAND]), ALU.mult))
            step(V.tensor_reduce(tab_f[:, 1:1 + MAX_EXTRA], prod, AX_X, ALU.add))
            step(V.tensor_reduce(tab_f[:, 0:1], is_extra[:, :], AX_X, ALU.add))
            step(V.tensor_scalar(tab_f[:, 0:1], tab_f[:, 0:1], float(N_EXPERTS), None, ALU.add))
            V.tensor_copy(table[0:1, :], tab_f[0:1, :]).then_inc(table_ready, 1)
            for d in range(KB):
                V.tensor_scalar(r[:, d, :], h[:, d, :], ALPHA, None, ALU.mult).then_inc(added, 1)
            dve.wait_ge(table_ready, 1)
            dve.wait_ge(gathered, 1)
            V.tensor_copy(xg[:, 0:4, :], bank[6][:, 0:4 * W].rearrange("p (k n) -> p k n", k=4)).then_inc(xg_dve, 1)
            n_items = dve.value_load(table[0:1, 0:1], min_val=N_EXPERTS, max_val=N_EXPERTS + MAX_EXTRA)
            with dve.Fori(0, n_items) as i:
                dve.wait_ge(gathered, i + 1)
                for t in range(TT):
                    rows = TILE_ROWS[t]
                    last = V.tensor_scalar(sel_w[0:rows, t, :], const("slot")[0:rows, :],
                                           item_pos[0:rows, t, bass.ds(i, 1)], item_gate[0:rows, t, bass.ds(i, 1)],
                                           ALU.is_equal, ALU.mult)
                last.then_inc(sel_w_ready, 1)
                for g in range(GROUPS):
                    dve.wait_ge(e_silu, i * GROUPS + g + 1)
                    dve.wait_ge(chunk_done, i * CPI + item_place["up", g] + 1)
                    if g >= 2:
                        dve.wait_ge(chunk_done, i * CPI + item_place["down", g - 2] + 1)
                    V.tensor_tensor(act_e[:, g % 2, :], gate_e[:, g % 2, :], bank[2 * (g % 2) + 1][:, 0:FPC * W],
                                    ALU.mult).then_inc(e_act, 1)
                    if g == 3:
                        select(sel, bass.ds(i + 1, 1), sel_ready)
                dve.wait_ge(chunk_done, i * CPI + CPI)
                V.tensor_copy(y_item[:, 0:4, :], bank[4][:, 0:4 * W].rearrange("p (k n) -> p k n", k=4)).then_inc(yi_dve, 1)
                dve.wait_ge(gathered, i + 2)
                V.tensor_copy(xg[:, 0:4, :], bank[6][:, 0:4 * W].rearrange("p (k n) -> p k n", k=4)).then_inc(xg_dve, 1)
                dve.wait_ge(y_turned, i * 2 + 1)
                V.tensor_copy(y_tok[0:W, 0:512], bank[4][0:W, :]).then_inc(yt_dve, 1)
                for d in range(KB):
                    dve.wait_ge(scattered, i * KB + d + 1)
                    V.tensor_tensor(r[:, d, :], r[:, d, :], bank[d % 4][:, 0:TOKENS], ALU.add).then_inc(added, 1)
            ln_centre("ffn1", r)
            ln_scale("ffn1", r)

        @block.gpsimd
        def _(pool):
            G = nc.gpsimd
            G.dma_start(vec[:, :], t_in["vec"]).then_inc(vec_in, 16)
            G.dma_start(cst[:, :], t_in["cst"]).then_inc(cst_in, 16)
            G.memset(w_pool[:, :, :, :], 0.0).then_inc(pool_set, 1)
            for layer in range(DEPTH):
                G.dma_start(ws_t[:, layer, :, :], t_in["ws_t"][layer].rearrange("h j i -> j h i")).then_inc(par_in, 16)
                G.dma_start(ws_s[:, layer, :, :], t_in["ws_s"][layer].rearrange("h j i -> j h i")).then_inc(par_in, 16)
                G.dma_start(bs[:, layer, :, :], t_in["bs_t"][layer].rearrange("(k p) t -> p k t", p=P)).then_inc(par_in, 16)
            G.dma_start(w_router[:, :, :], t_in["w_router"][0].rearrange("(k p) e -> p k e", p=P)).then_inc(par_in, 16)
            pool.wait_ge(pool_set, 1)
            for layer in range(DEPTH):
                for half in range(2):
                    lo = 64 * half
                    G.dma_start(w_pool[lo:lo + 64, layer, :, lo:lo + 64],
                                t_in["w_pool"][layer].rearrange("(b two) c d -> two c b d", two=2)[half]).then_inc(par_in, 16)

            def load_past(layer):
                for ext, past, src, done in ((ext_a, PAST_A, "past_a", past_a), (ext_c, PAST_C, "past_c", past_c),
                                             (ext_d, POOL_PAST, "past_d", past_d)):
                    for b in range(MB):
                        v = samples_of(ext, b, past, 0, past)
                        s = t_in[src][layer, b * P:(b + 1) * P]
                        for half in range(2):
                            lo = 4 * half
                            G.dma_start(v[:, lo:lo + 4, :], s[:, lo:lo + 4, :]).then_inc(done, 16)

            load_past(0)
            pool.wait_ge(par_in, PARAMS * 16)
            for layer in range(DEPTH):
                G.affine_select(out=ws_t[:, layer, :, :], in_=ws_t[:, layer, :, :], compare_op=ALU.is_ge, fill=0.0,
                                base=0, pattern=[[0, HEADS], [1, CHUNK]], channel_multiplier=-1)
            w4 = ws_s[:, :, :, :].rearrange("p l h i -> p (l h) i")
            G.affine_select(out=w4, in_=w4, compare_op=ALU.is_ge, fill=0.0, base=0,
                            pattern=[[0, DEPTH * HEADS], [1, N_SAMPLE]], channel_multiplier=-1).then_inc(pool_set, 1)
            pool.wait_ge(pool_set, 2)
            w5 = ws_s[:, :, :, :].rearrange("p l h (s i) -> p (l h) s i", s=DEC_BATCH)
            G.affine_select(out=w5, in_=w5, compare_op=ALU.is_ge, fill=0.0, base=0,
                            pattern=[[0, DEPTH * HEADS], [-DEC_SEQ, DEC_BATCH], [0, DEC_SEQ]],
                            channel_multiplier=1).then_inc(setup, 1)

            def layer_norm_root(name):
                n = LNS.index(name)
                pool.wait_ge(ln_ve, n + 1)
                G.tensor_tensor(rstd_tok[:, :], var_tok[:, :], minus_half[:, :], ALU.pow).then_inc(ln_rs, 1)

            def pooling(layer):
                base = 8 * layer
                pool.wait_ge(past_d, 64 * (layer + 1))
                pool.wait_ge(z_act, 10 * layer + 8)
                n = LEN_D

                def add(dst, src, p0, b0, shift, lo):
                    return G.tensor_tensor(dst[p0:P, b0:MB, lo:n], src[p0:P, b0:MB, lo:n],
                                           src[p0:P, b0:MB, lo - shift:n - shift], ALU.add)

                add(sum_a, ext_d, 0, 0, 1, 1).then_inc(pool_step, 1)
                pool.wait_ge(pool_step, base + 1)
                add(sum_b, sum_a, 0, 0, 2, 3).then_inc(pool_step, 1)
                pool.wait_ge(pool_step, base + 2)
                add(sum_a, sum_b, 0, 1, 4, 7).then_inc(pool_step, 1)
                pool.wait_ge(pool_step, base + 3)
                add(sum_b, sum_a, 64, 1, 8, 15).then_inc(pool_step, 1)
                pool.wait_ge(pool_step, base + 4)
                inv = const("inv_count", MB)
                for lo, s in ((0, sum_a), (64, sum_b)):
                    hi = lo + 64
                    G.tensor_tensor(dd[lo:hi, :, 0:SEQ], s[lo:hi, :, POOL_PAST:POOL_PAST + SEQ],
                                    inv[lo:hi, :, 0:SEQ], ALU.mult)
                    for b in range(MB):
                        last = G.tensor_tensor(sample_cols(dd[:, b, :])[lo:hi],
                                               samples_of(s, b, POOL_PAST, POOL_PAST, POOL_PAST + DEC_SEQ)[lo:hi],
                                               sample_cols(inv[:, b, :])[lo:hi], ALU.mult)
                    last.then_inc(pool_step, 1)
                pool.wait_ge(pool_step, base + 6)
                G.tensor_tensor(dd[:, :, 0:SEQ], dd[:, :, 0:SEQ], ext_d[:, :, POOL_PAST:POOL_PAST + SEQ],
                                ALU.subtract).then_inc(pool_step, 1)
                for b in range(MB):
                    last = G.tensor_tensor(sample_cols(dd[:, b, :]), sample_cols(dd[:, b, :]),
                                           samples_of(ext_d, b, POOL_PAST, POOL_PAST, POOL_PAST + DEC_SEQ), ALU.subtract)
                last.then_inc(pool_step, 1)

            def store_rows(layer, ext, past, name, done):
                for b in range(MB):
                    G.dma_start(t_out[name + "_p"][layer, b * P:(b + 1) * P], ext[:, b, SEQ:SEQ + past]).then_inc(done, 16)
                    G.dma_start(t_out[name + "_s"][layer, b * P:(b + 1) * P],
                                samples_of(ext, b, past, DEC_SEQ, DEC_SEQ + past)).then_inc(done, 16)

            layer_norm_root("in")
            pool.wait_ge(cst_in, 16)
            pool.wait_ge(ones_ready, 2)
            for layer in range(DEPTH):
                pooling(layer)
                pool.wait_ge(z_dve, 6 * layer + 2)
                store_rows(layer, ext_a, PAST_A, "conv_a", st_a)
                store_rows(layer, ext_d, POOL_PAST, "pool_d", st_d)
                layer_norm_root(f"v{layer}")
                layer_norm_root(f"a{layer}")
                pool.wait_ge(z_dve, 6 * layer + 4)
                store_rows(layer, ext_c, PAST_C, "conv_c", st_c)
                pool.wait_ge(ln_out, LN_AT[f"v{layer}"] + MB)
                for b in range(MB):
                    G.dma_start(t_out["v_p"][layer, b * P:(b + 1) * P], vn[:, b, SEQ - CHUNK:SEQ]).then_inc(st_v, 16)
                    G.dma_start(t_out["v_s"][layer, b * P:(b + 1) * P], vn[:, b, SEQ:TOKENS]).then_inc(st_v, 16)
                if layer + 1 < DEPTH:
                    pool.wait_ge(z_dve, 6 * layer + 6)
                    for s in (st_a, st_c, st_d):
                        pool.wait_ge(s, 64 * (layer + 1))
                    load_past(layer + 1)
                layer_norm_root(f"mix{layer}")
                layer_norm_root(f"ffn{layer}")
            for s in (st_a, st_c, st_d, st_v):
                pool.wait_ge(s, 64 * DEPTH)


PARAMS = 3 * DEPTH + 1 + 2 * DEPTH

_OUTS = {"y_t": (D_MODEL, TOKENS), "conv_a_p": (DEPTH, MB * P, PAST_A), "conv_a_s": (DEPTH, MB * P, DEC_BATCH, PAST_A),
         "conv_c_p": (DEPTH, MB * P, PAST_C), "conv_c_s": (DEPTH, MB * P, DEC_BATCH, PAST_C),
         "pool_d_p": (DEPTH, MB * P, POOL_PAST), "pool_d_s": (DEPTH, MB * P, DEC_BATCH, POOL_PAST),
         "v_p": (DEPTH, MB * P, CHUNK), "v_s": (DEPTH, MB * P, N_SAMPLE)}


def constants():
    c = {}
    c["ident"] = np.eye(P)
    c["before"] = np.triu(np.ones((P, P)), 1)
    window = np.array([2, 4, 8, 16]).repeat(64).reshape(MB, P).T
    pos = np.concatenate([np.arange(SEQ), np.full(N_SAMPLE, SEQ)])
    c["inv_count"] = 1.0 / np.minimum(pos[None, None, :] + 1.0, window[:, :, None])
    c["slot"] = np.tile(np.arange(W), (P, 1))
    c["rank8"] = np.tile(N_EXPERTS - np.arange(N_EXPERTS), (P, 1))
    c["valid"] = np.stack([np.arange(P) < n for n in TILE_ROWS], 1)
    c["extra_no"] = np.tile(np.arange(MAX_EXTRA), (P, 1))
    c["earlier"] = np.tile(np.tril(np.ones((CAND, CAND)), -1).reshape(-1), (P, 1))
    c["cand_expert"] = np.tile(np.arange(CAND) % N_EXPERTS, (P, 1))
    c["cand_level"] = np.tile(np.arange(CAND) // N_EXPERTS, (P, 1))
    return np.concatenate([c[n].reshape(P, size) for n, size in CST], axis=1).astype(np.float32)


def kernel(**inputs):
    import concourse.bacc as _bacc
    from concourse.bass_utils import run_bass_kernel_spmd as _run

    x = {k: np.asarray(v) for k, v in inputs.items()}
    arrays = {"cst": constants()}
    rows = np.concatenate([x["x_prompt"].reshape(SEQ, D_MODEL), x["x_sample"].reshape(N_SAMPLE, D_MODEL)])
    arrays["x_t"] = rows.T
    vecs = [x["ln_in_g"].reshape(-1, P), x["ln_in_b"].reshape(-1, P)]
    for layer in range(DEPTH):
        vecs += [x[name][layer].reshape(-1, P) for name, _ in VEC]
    arrays["vec"] = np.concatenate(vecs).T
    for name, src in (("past_a", "state_conv_a"), ("past_c", "state_conv_c"), ("past_d", "state_pool_d")):
        arrays[name] = x[src].transpose(0, 3, 1, 2)
    arrays["ws_t"] = x["w_s"].transpose(0, 1, 3, 2)
    arrays["ws_s"] = np.tile(x["w_s"][:, :, :DEC_SEQ, :DEC_SEQ].transpose(0, 1, 3, 2), (1, 1, DEC_BATCH, DEC_BATCH))
    bias = np.concatenate([x["b_s"], x["b_s"], np.tile(x["b_s"][:, :, :DEC_SEQ], (1, 1, DEC_BATCH))], axis=2)
    arrays["bs_t"] = bias.repeat(MB * P // HEADS, axis=1)
    for name in ("w_in", "w_out", "w_pool", "w_router", "w_ff_gate", "w_ff_up", "w_ff_down", "w_e_gate", "w_e_up", "w_e_down"):
        arrays[name] = x[name]

    nc = _bacc.Bacc("TRN2", target_bir_lowering=False, num_devices=1)
    arrays = {f"in_{k}": np.ascontiguousarray(v) for k, v in arrays.items()}
    t_in = {k[3:]: nc.dram_tensor(k, v.shape, F32, kind="ExternalInput").ap() for k, v in arrays.items()}
    t_out = {k: nc.dram_tensor(f"out_{k}", s, F32, kind="ExternalOutput").ap() for k, s in _OUTS.items()}
    build(nc, t_in, t_out)
    got = _run(nc, [arrays], core_ids=[0]).results[0]

    y = got["out_y_t"].T
    y_prompt = y[:SEQ].reshape(1, SEQ, D_MODEL)
    y_sample = y[SEQ:].reshape(DEC_BATCH, DEC_SEQ, D_MODEL)

    def prompt_rows(name):
        return got[f"out_{name}_p"].transpose(0, 2, 1)[:, None]

    def sample_rows(name):
        return got[f"out_{name}_s"].transpose(0, 2, 3, 1)

    v_s = got["out_v_s"].transpose(0, 2, 1).reshape(DEPTH, DEC_BATCH, DEC_SEQ, MB * P)
    out = (y_prompt, y_sample, prompt_rows("conv_a"), prompt_rows("conv_c"), prompt_rows("pool_d"), prompt_rows("v"),
           sample_rows("conv_a"), sample_rows("conv_c"), sample_rows("pool_d"), v_s)
    return tuple(np.ascontiguousarray(o) for o in out)
```

```python
from contextlib import ExitStack

import numpy as np

import concourse.bass as bass
from concourse import mybir

ALU = mybir.AluOpType
ACT = mybir.ActivationFunctionType
AX_X = mybir.AxisListType.X
F32 = mybir.dt.float32
F32R = mybir.dt.float32r
I32 = mybir.dt.int32

P = 128
DEPTH, D_MODEL, SEQ, DEC_BATCH, DEC_SEQ = 2, 1024, 256, 8, 4
N_SAMPLE = DEC_BATCH * DEC_SEQ
TOKENS = SEQ + N_SAMPLE
KB = D_MODEL // P
MB = 2
TAPS_A, TAPS_C, POOL_PAST = 31, 3, 15
PAST_A, PAST_C = TAPS_A - 1, TAPS_C - 1
HEADS, CHUNK = 4, 128
D_FF, N_EXPERTS = 3584, 8
FB = D_FF // P
ALPHA = (2.0 * DEPTH) ** 0.25
LN_EPS = 1e-5
TT = 3
TILE_ROWS = [P, P, TOKENS - 2 * P]

SLOTS = 6
SPLIT = 3
FPC = 2
CH = KB * FPC * P
GROUPS = FB // FPC
GC = 512
E_GROUPS = D_FF // GC
GB = GC // P
CPI = 6 * E_GROUPS
assert CPI % SLOTS == 0 and CPI % SPLIT == 0

W = 128
MAX_EXTRA = 2 * TOKENS // (W + 1)
LEVELS = (TOKENS - 1) // W
CAND = LEVELS * N_EXPERTS
N_ITEMS = N_EXPERTS + MAX_EXTRA + 1

LEN_A = PAST_A + SEQ + DEC_BATCH * (PAST_A + DEC_SEQ)
LEN_C = PAST_C + SEQ + DEC_BATCH * (PAST_C + DEC_SEQ)
LEN_D = POOL_PAST + SEQ + DEC_BATCH * (POOL_PAST + DEC_SEQ)

VEC = [("conv_a_w", TAPS_A * MB), ("conv_a_b", MB), ("ln_a_g", MB), ("ln_a_b", MB), ("ln_v_g", MB),
       ("ln_v_b", MB), ("conv_c_w", TAPS_C * MB), ("pool_scale", MB), ("ln_mix_g", KB),
       ("ln_mix_b", KB), ("ln_ffn_g", KB), ("ln_ffn_b", KB)]
VEC_LAYER = sum(n for _, n in VEC)
VEC_ALL = 2 * KB + DEPTH * VEC_LAYER

CST = [("ident", P), ("before", P), ("inv_count", MB * TOKENS), ("slot", W), ("rank8", N_EXPERTS),
       ("valid", TT), ("extra_no", MAX_EXTRA), ("earlier", CAND * CAND), ("cand_expert", CAND)]
CST_ALL = sum(n for _, n in CST)

Z_BLOCKS = [2, 3, 0, 1, 6, 7, 4, 5, 14, 15, 12, 13, 8, 9, 10, 11]
Z_CHUNKS = [n // FPC for n in Z_BLOCKS[::FPC]]
Z_BY_ACT = [0, 1, 4, 5, 6, 7, 8, 9, 10, 11]
Z_BY_DVE = [2, 3, 12, 13, 14, 15]
LNS = ["in", "v0", "a0", "mix0", "ffn0", "v1", "a1", "mix1", "ffn1"]
LN_BLOCKS = {n: (MB if n[0] in "va" else KB) for n in LNS}
LN_AT = {n: sum(LN_BLOCKS[m] for m in LNS[:i]) for i, n in enumerate(LNS)}


def vec_at(name, layer=None):
    if layer is None:
        return {"ln_in_g": 0, "ln_in_b": KB}[name]
    at = 2 * KB + layer * VEC_LAYER
    for n, size in VEC:
        if n == name:
            return at
        at += size
    raise KeyError(name)


def cst_at(name):
    at = 0
    for n, size in CST:
        if n == name:
            return at, size
        at += size
    raise KeyError(name)


def build(nc, t_in, t_out):
    ctx = ExitStack()
    with ctx:
        def sb(name, shape, dt=F32):
            return ctx.enter_context(nc.sbuf_tensor(name, shape, dt))

        def sem(name):
            return ctx.enter_context(nc.semaphore(name))

        ring = [sb(f"ring{i}", [P, CH]) for i in range(SLOTS)]
        w_hi = [sb(f"w_hi{i}", [P, CH], F32R) for i in range(SPLIT)]
        w_lo = [sb(f"w_lo{i}", [P, CH], F32R) for i in range(SPLIT)]
        x_hi = sb("x_hi", [P, KB, TOKENS], F32R)
        x_lo = sb("x_lo", [P, KB, TOKENS], F32R)
        ad_hi = sb("ad_hi", [P, 2 * TOKENS], F32R)
        ad_lo = sb("ad_lo", [P, 2 * TOKENS], F32R)
        a_hi = ad_hi[:, 0:GB * W].rearrange("p (f n) -> p f n", f=GB)
        a_lo = ad_lo[:, 0:GB * W].rearrange("p (f n) -> p f n", f=GB)
        h = sb("h", [P, KB, TOKENS])
        r = sb("r", [P, KB, TOKENS])
        ybuf = sb("ybuf", [P, KB * TOKENS])
        ext_a = sb("ext_a", [P, MB, LEN_A])
        ext_c = sb("ext_c", [P, MB, LEN_C])
        ext_d = sb("ext_d", [P, MB, LEN_D])
        work = sb("work", [P, FB * TOKENS])
        vec = sb("vec", [P, VEC_ALL])
        cst = sb("cst", [P, CST_ALL])
        ones = sb("ones", [P, P])
        ones_mix = sb("ones_mix", [P, P])
        ones_model = sb("ones_model", [P, P])
        ws_t = sb("ws_t", [P, DEPTH, HEADS, CHUNK])
        ws_s = sb("ws_s", [N_SAMPLE, DEPTH, HEADS, N_SAMPLE])
        bs = sb("bs", [P, DEPTH, MB, TOKENS])
        w_pool = sb("w_pool", [P, DEPTH, MB, P])
        w_router = sb("w_router", [P, KB, N_EXPERTS])
        scat = sb("scat", [P, TOKENS], F32R)
        var_tok = sb("var_tok", [P, TT])
        rstd_tok = sb("rstd_tok", [P, TT])
        minus_half = sb("minus_half", [P, TT])
        table = sb("table", [1, 1 + MAX_EXTRA], I32)
        bank = [ctx.enter_context(nc.psum_tensor(f"bank{i}", [P, 512], F32)) for i in range(8)]

        def part(buf, at, *dims):
            n = int(np.prod(dims))
            v = buf[:, at:at + n]
            if len(dims) == 2:
                v = v.rearrange("p (a b) -> p a b", a=dims[0])
            if len(dims) == 3:
                v = v.rearrange("p (a b c) -> p a b c", a=dims[0], b=dims[1])
            return v, at + n

        at = 0
        acc_a, at = part(work, at, MB, TOKENS)
        sig, at = part(work, at, MB, TOKENS)
        gv, at = part(work, at, MB, TOKENS)
        vn, at = part(work, at, MB, TOKENS)
        gu, at = part(work, at, MB, TOKENS)
        cc, at = part(work, at, MB, TOKENS)
        sq_s, at = part(work, at, MB, TOKENS)
        acc_c, at = part(work, at, MB, LEN_C)
        sum_a, at = part(work, at, MB, LEN_D)
        sum_b, at = part(work, at, MB, LEN_D)
        v_tok, at = part(work, at, TT, MB * P)
        assert at <= FB * TOKENS
        dd = sig
        y = ybuf[:, :].rearrange("p (k t) -> p k t", k=KB)
        sq_l = y
        diag_l, _ = part(ybuf, 0, TT, P)
        diag_s = sq_s.rearrange("p b t -> p (b t)")[:, 0:TT * P].rearrange("p (t n) -> p t n", t=TT)
        n_prod = DEC_BATCH * DEC_SEQ * TAPS_A
        prod_s = [ybuf[:, b * n_prod:(b + 1) * n_prod].rearrange("p (s l t) -> p s l t", s=DEC_BATCH, l=DEC_SEQ)
                  for b in range(MB)]
        act_d = work[:, :].rearrange("p (f t) -> p f t", f=FB)
        gate_d, _ = part(ybuf, 0, 2, TOKENS)
        at = 0
        h_tok, at = part(work, at, TT, D_MODEL)
        gate_e, at = part(work, at, 2, GC)
        sel, at = part(work, at, TT, W)
        sel_w, at = part(work, at, TT, W)
        at = 0
        y_hi, y_lo = x_hi[:, :, W:2 * W], x_lo[:, :, W:2 * W]
        slot_gate, at = part(ybuf, at, 1)
        item_pos, at = part(ybuf, at, TT, N_ITEMS)
        item_gate, at = part(ybuf, at, TT, N_ITEMS)
        logit, at = part(ybuf, at, TT, N_EXPERTS)
        key, at = part(ybuf, at, TT, N_EXPERTS)
        hot1, at = part(ybuf, at, TT, N_EXPERTS)
        hot2, at = part(ybuf, at, TT, N_EXPERTS)
        chosen, at = part(ybuf, at, TT, N_EXPERTS)
        cand_pos, at = part(ybuf, at, TT, CAND)
        cand_gate, at = part(ybuf, at, TT, CAND)
        col, at = part(ybuf, at, 8, TT)
        counts, at = part(ybuf, at, N_EXPERTS)
        is_extra, at = part(ybuf, at, CAND)
        extra_rank, at = part(ybuf, at, CAND)
        picked, at = part(ybuf, at, MAX_EXTRA, CAND)
        tmp, at = part(ybuf, at, max(MAX_EXTRA, CAND) * CAND)
        tab_f, at = part(ybuf, at, 1 + MAX_EXTRA)
        assert at <= KB * TOKENS

        def const(name, dims=None):
            a, n = cst_at(name)
            v = cst[:, a:a + n]
            return v.rearrange("p (a b) -> p a b", a=dims) if dims else v

        ident = const("ident")
        before = const("before")

        ring_in = [sem(f"ring_in{i}") for i in range(SLOTS)]
        x_in, vec_in, cst_in, par_in = sem("x_in"), sem("vec_in"), sem("cst_in"), sem("par_in")
        w_pool_in = sem("w_pool_in")
        past_a, past_c, past_d = sem("past_a"), sem("past_c"), sem("past_d")
        ones_ready, setup = sem("ones_ready"), sem("setup")
        pool_set = sem("pool_set")
        ln_mean, ln_xc, ln_sq, ln_var = sem("ln_mean"), sem("ln_xc"), sem("ln_sq"), sem("ln_var")
        ln_ve, ln_rs, ln_xn, ln_out = sem("ln_ve"), sem("ln_rs"), sem("ln_xn"), sem("ln_out")
        ln_spread = sem("ln_spread")
        z_ready, z_act, z_dve = sem("z_ready"), sem("z_act"), sem("z_dve")
        conv_a, conv_c = sem("conv_a"), sem("conv_c")
        v_turned, v_tok_act = sem("v_turned"), sem("v_tok_act")
        mixed_b, b_sum, y_b = sem("mixed_b"), sem("b_sum"), sem("y_b")
        pool_step, mapped_d, y_d = sem("pool_step"), sem("mapped_d"), sem("y_d")
        proj_ready, r_ready = sem("proj_ready"), sem("r_ready")
        gate_ready, up_ready, silu_done, act_done = (sem("gate_ready"), sem("up_ready"),
                                                     sem("silu_done"), sem("act_done"))
        down_chunk = sem("down_chunk")
        st_a, st_c, st_d, st_v, st_y = sem("st_a"), sem("st_c"), sem("st_d"), sem("st_v"), sem("st_y")
        logits_ready, h_turned, h_tok_dve, h_tok_act = (sem("logits_ready"), sem("h_turned"),
                                                        sem("h_tok_dve"), sem("h_tok_act"))
        route, exp_done, chosen_ready, pos_ready = (sem("route"), sem("exp_done"),
                                                    sem("chosen_ready"), sem("pos_ready"))
        table_ready, chosen_top = sem("table_ready"), sem("chosen_top")
        chunk_done = sem("chunk_done")
        act_hi_done, act_lo_done = sem("act_hi_done"), sem("act_lo_done")
        in_hi_done, in_lo_done = sem("in_hi_done"), sem("in_lo_done")
        prods, summed_s = sem("prods"), sem("summed_s")
        hi_done, lo_done = sem("hi_done"), sem("lo_done")
        sel_ready, sel_w_ready, gathered = sem("sel_ready"), sem("sel_w_ready"), sem("gathered")
        x_hi_done, x_lo_done = sem("x_hi_done"), sem("x_lo_done")
        sel_turned, scat_ready = sem("sel_turned"), sem("scat_ready")
        e_silu, e_act, a_turned = sem("e_silu"), sem("e_act"), sem("a_turned")
        a_hi_done, a_lo_done = sem("a_hi_done"), sem("a_lo_done")
        y_lo_done, y_hi_done, scattered, added = (sem("y_lo_done"), sem("y_hi_done"), sem("scattered"),
                                            sem("added"))

        def prompt_of(ext, b, past):
            return ext[:, b, past:past + SEQ]

        def samples_of(ext, b, past, lo, hi):
            return ext[:, b, past + SEQ:].rearrange("p (s l) -> p s l", s=DEC_BATCH)[:, :, lo:hi]

        def sample_cols(v):
            return v[:, SEQ:TOKENS].rearrange("p (s l) -> p s l", s=DEC_BATCH)

        def in_chunk(w, c):
            return w[:, c * FPC * P:(c + 1) * FPC * P].rearrange("(k p) n -> p k n", p=P)

        def down_rows(w, c):
            return w[c * FPC * P:(c + 1) * FPC * P, :].rearrange("(k p) n -> p k n", p=P)

        stream = []
        proj_uses = 0
        for layer in range(DEPTH):
            for j, c in enumerate(Z_CHUNKS):
                stream.append((in_chunk(t_in["w_in"][layer], c), z_ready, 16 * layer + FPC * (j + 1)))
            for j in range(KB // FPC):
                stream.append((in_chunk(t_in["w_out"][layer], j), proj_ready, KB * proj_uses + FPC * (j + 1)))
            proj_uses += 1
            if layer == 0:
                for g in range(GROUPS):
                    stream.append((in_chunk(t_in["w_ff_gate"][0], g), gate_ready, FPC * (g + 1)))
                    stream.append((in_chunk(t_in["w_ff_up"][0], g), up_ready, FPC * (g + 1)))
                for g in range(GROUPS):
                    done = (down_chunk, FPC * (g + 1)) if g < GROUPS - 1 else (proj_ready, 8 * proj_uses + 8)
                    stream.append((down_rows(t_in["w_ff_down"][0], g), *done))
                proj_uses += 1
        START = len(stream)
        DENSE_AT = len(Z_CHUNKS) + KB // FPC
        DOWN_AT = DENSE_AT + 2 * GROUPS
        item_chunks = []
        for g in range(E_GROUPS + 1):
            if g < E_GROUPS:
                item_chunks += [("gate", g, 0), ("gate", g, 1), ("up", g, 0), ("up", g, 1)]
            if g:
                item_chunks += [("down", g - 1, 0), ("down", g - 1, 1)]
        item_place = {c: p for p, c in enumerate(item_chunks)}

        def arrived(eng, c):
            eng.wait_ge(ring_in[c % SLOTS], 16 * (c // SLOTS + 1))

        def item_arrived(eng, i, p):
            c = START + p
            eng.wait_ge(ring_in[c % SLOTS], i * (16 * CPI // SLOTS) + 16 * (c // SLOTS + 1))

        def slot_of(c):
            return ring[c % SLOTS][:, :].rearrange("p (k n) -> p k n", n=FPC * P)

        def down_of(c):
            return ring[c % SLOTS][:, :].rearrange("p (k n) -> p k n", n=D_MODEL)

        def before_split(p):
            return [(kind, g) for g in range(E_GROUPS) for kind, at in (
                ("silu", item_place["up", g, 1] + 2),
                ("act", item_place["up", g, 1] + 3),
                ("parts", item_place["gate", g + 1, 1] + 3 if g + 1 < E_GROUPS else CPI),
            ) if min(at, CPI) == p]

        SCATTER_BANKS = [2, 6, 7, 1, 4, 5, 3, 2]
        CUT_AHEAD = 2

        def in_cuts(stage):
            return KB * ["in", "y0", "mix0", "ffn0", "y1"].index(stage)

        Y_ORDER = [6, 7, 4, 5, 2, 3, 0, 1]

        block = ctx.enter_context(nc.Block())

        @block.sync
        def _(sp):
            xt = t_in["x_t"].rearrange("(k p) t -> p k t", p=P)
            for half in range(2):
                sp.dma_start(h[:, 4 * half:4 * half + 4, :], xt[:, 4 * half:4 * half + 4, :]).then_inc(x_in, 16)
            sp.dma_start(vec[:, :], t_in["vec"]).then_inc(vec_in, 16)
            sp.dma_start(cst[:, :], t_in["cst"]).then_inc(cst_in, 16)
            for c, (src, _, _) in enumerate(stream):
                if c >= SLOTS:
                    sp.wait_ge(lo_done, c - SLOTS + 1)
                slot = down_of(c) if src.shape[2] == D_MODEL else slot_of(c)
                sp.dma_start(slot, src).then_inc(ring_in[c % SLOTS], 16)

            names = {"gate": "w_e_gate", "up": "w_e_up", "down": "w_e_down"}

            def load_item(i, expert):
                for p, (kind, g, half) in enumerate(item_chunks):
                    c = START + p
                    sp.wait_ge(lo_done, i * CPI + (c - SLOTS + 1))
                    w = t_in[names[kind]][0]
                    if kind == "down":
                        rows = GC // 2
                        at = g * GC + half * rows
                        src = w[bass.ds(expert, 1), at:at + rows, :]
                        slot = down_of(c)
                    else:
                        rows = D_MODEL // 2
                        src = w[bass.ds(expert, 1), half * rows:(half + 1) * rows, g * GC:(g + 1) * GC]
                        slot = ring[c % SLOTS][:, :].rearrange("p (k n) -> p k n", n=GC)
                    src = src.rearrange("e (k p) n -> p (e k) n", p=P)
                    sp.dma_start(slot, src).then_inc(ring_in[c % SLOTS], 16)

            with sp.Fori(0, N_EXPERTS) as i:
                load_item(i, i)
            sp.wait_ge(table_ready, 1)
            n_items = sp.value_load(table[0:1, 0:1], min_val=N_EXPERTS, max_val=N_EXPERTS + MAX_EXTRA)
            with sp.If(n_items > N_EXPERTS):
                with sp.Fori(N_EXPERTS, n_items) as i:
                    expert = sp.value_load(table[0:1, bass.ds(i - (N_EXPERTS - 1), 1)],
                                           min_val=0, max_val=N_EXPERTS - 1)
                    load_item(i, expert)
            y_out = t_out["y_t"].rearrange("(k p) t -> p k t", p=P)
            for half in range(2):
                sp.wait_ge(ln_out, LN_AT["ffn1"] + 4 * (half + 1))
                sp.dma_start(y_out[:, 4 * half:4 * half + 4, :], h[:, 4 * half:4 * half + 4, :]).then_inc(st_y, 16)
            sp.wait_ge(st_y, 32)

        @block.tensor
        def _(pe):
            mm = nc.tensor.matmul

            def ln_sums(name, x, sq, weights, ready):
                n, nb = LNS.index(name), LN_BLOCKS[name]
                for b in range(nb):
                    ready(b)
                    last = mm(bank[6][:, 0:TOKENS], weights[:, :], x[:, b, :], start=(b == 0), stop=(b == nb - 1))
                last.then_inc(ln_mean, 1)
                yield
                for b in range(nb):
                    pe.wait_ge(ln_sq, LN_AT[name] + b + 1)
                    last = mm(bank[7][:, 0:TOKENS], weights[:, :], sq[:, b, :], start=(b == 0), stop=(b == nb - 1))
                last.then_inc(ln_var, 1)
                yield
                pe.wait_ge(ln_rs, n + 1)
                if name == "in":
                    pe.wait_ge(cst_in, 16)
                for t in range(TT):
                    rows = TILE_ROWS[t]
                    last = mm(bank[7][:, t * P:t * P + rows], rstd_tok[0:rows, t:t + 1].broadcast_to([rows, P]),
                              ident[0:rows, 0:rows], start=True, stop=True)
                last.then_inc(ln_spread, 1)
                yield

            def large_ln(name, ready):
                for _ in ln_sums(name, r if name != "in" else h, sq_l, ones_model, ready):
                    pass

            def w_parts(out, c, at, hi, lo, first, last):
                w1, w2 = w_hi[c % SPLIT][:, at:at + P], w_lo[c % SPLIT][:, at:at + P]
                for n, (w, x) in enumerate(((w1, hi), (w1, lo), (w2, hi))):
                    ins = mm(out, w, x, start=(first and n == 0), stop=(last and n == 2), skip_group_check=True)
                return ins

            def z_block(layer, n, c0):
                if n % FPC == 0:
                    pe.wait_ge(lo_done, c0 + n // FPC + 1)
                if n >= 6:
                    if n - 6 in Z_BY_ACT:
                        pe.wait_ge(z_act, len(Z_BY_ACT) * layer + Z_BY_ACT.index(n - 6) + 1)
                    else:
                        pe.wait_ge(z_dve, len(Z_BY_DVE) * layer + Z_BY_DVE.index(n - 6) + 1)
                at = Z_BLOCKS[n] % FPC * P
                for k in range(KB):
                    if n == 0:
                        pe.wait_ge(in_lo_done, in_cuts("ffn0" if layer else "in") + k + 1)
                    last = w_parts(bank[n % 6][:, 0:TOKENS], c0 + n // FPC, k * FPC * P + at, x_hi[:, k, :],
                                   x_lo[:, k, :], k == 0, k == KB - 1)
                last.then_inc(z_ready, 1)

            def mixer(layer, c0):
                name_v, name_a = f"v{layer}", f"a{layer}"
                ln_v = ln_sums(name_v, gv, sq_s, ones_mix,
                               lambda b: pe.wait_ge(z_act, 10 * layer + 3 + b))
                ln_a = ln_sums(name_a, acc_a, sq_s, ones_mix,
                               lambda b: (pe.wait_ge(conv_a, MB * TAPS_A * (layer + 1)),
                                          pe.wait_ge(summed_s, 2 * MB * (layer + 1))))
                for n in range(8):
                    z_block(layer, n, c0)
                next(ln_v)
                for n in range(8, 11):
                    z_block(layer, n, c0)
                next(ln_v)
                for n in range(11, 13):
                    z_block(layer, n, c0)
                next(ln_v)
                z_block(layer, 13, c0)
                pe.wait_ge(ln_out, LN_AT[name_v] + MB)
                for t in range(2):
                    for b in range(MB):
                        last = nc.tensor.transpose(bank[6][:, t * 256 + b * P:t * 256 + (b + 1) * P],
                                                   vn[:, b, t * P:(t + 1) * P], ident)
                last.then_inc(v_turned, 1)
                for b in range(MB):
                    last = nc.tensor.transpose(bank[7][0:N_SAMPLE, b * P:(b + 1) * P], vn[:, b, SEQ:TOKENS], ident)
                last.then_inc(v_turned, 1)
                for n in range(14, 16):
                    z_block(layer, n, c0)
                pe.wait_ge(w_pool_in, 2 * DEPTH * 16)
                for b in range(MB):
                    pe.wait_ge(pool_step, 8 * (layer + 1))
                    pe.wait_ge(z_act, 10 * (layer + 1))
                    mm(bank[4 + b][:, 0:TOKENS], w_pool[:, layer, b, :], dd[:, b, :],
                       start=True, stop=True).then_inc(mapped_d, 1)
                pe.wait_ge(v_tok_act, 2 * (layer + 1))
                next(ln_a)
                pe.wait_ge(setup, 1)
                pe.wait_ge(par_in, PARAMS * 16)
                pe.wait_ge(z_dve, len(Z_BY_DVE) * layer + 4)
                for b in range(MB):
                    for half in range(2):
                        head, lo = 2 * b + half, 64 * half
                        for t in range(2):
                            mm(bank[b][lo:lo + 64, t * P:(t + 1) * P], v_tok[:, t, head * 64:head * 64 + 64],
                               ws_t[:, layer, head, :], start=True, stop=True)
                        last = mm(bank[b][lo:lo + 64, SEQ:TOKENS], v_tok[0:N_SAMPLE, 2, head * 64:head * 64 + 64],
                                  ws_s[:, layer, head, :], start=True, stop=True)
                    last.then_inc(mixed_b, 1)
                next(ln_a)
                c1 = c0 + len(Z_CHUNKS)

                def project(d, blocks):
                    pe.wait_ge(lo_done, c1 + d // FPC + 1)
                    for j in blocks:
                        pe.wait_ge(in_lo_done, in_cuts(f"y{layer}") + j + 1)
                        k = Y_ORDER[j]
                        last = w_parts(bank[(6 + d) % 8][:, 0:TOKENS], c1 + d // FPC, k * FPC * P + d % FPC * P,
                                       x_hi[:, k, :], x_lo[:, k, :], j == 0, j == KB - 1)
                    return last

                EARLY = (4, 5, 2, 3)
                pe.wait_ge(z_dve, len(Z_BY_DVE) * (layer + 1))
                for d in EARLY[:2]:
                    project(d, range(6))
                next(ln_a)
                for d in EARLY[2:]:
                    project(d, range(6))
                pe.wait_ge(ln_xn, LN_AT[name_a] + MB)
                for d in range(KB):
                    project(d, range(6, KB) if d in EARLY else range(KB)).then_inc(proj_ready, 1)
                return c1 + KB // FPC

            def dense(c0):
                for g in range(GROUPS):
                    for which, ready in ((0, gate_ready), (1, up_ready)):
                        c = c0 + 2 * g + which
                        pe.wait_ge(lo_done, c + 1)
                        for f in range(FPC * g, FPC * (g + 1)):
                            if f >= 3 and which == 0:
                                pe.wait_ge(act_done, f - 2)
                            for k in range(KB):
                                if g == 0:
                                    pe.wait_ge(in_lo_done, in_cuts("mix0") + k + 1)
                                last = w_parts(bank[2 * (f % 3) + which][:, 0:TOKENS], c,
                                               k * FPC * P + f % FPC * P, x_hi[:, k, :], x_lo[:, k, :],
                                               k == 0, k == KB - 1)
                            last.then_inc(ready, 1)
                c0 += 2 * GROUPS
                pe.wait_ge(act_done, FB)
                for f in range(FB):
                    c = c0 + f // FPC
                    if f % FPC == 0:
                        pe.wait_ge(lo_done, c + 1)
                    pe.wait_ge(act_lo_done, f + 1)
                    at = f % 2 * TOKENS
                    for d in range(KB):
                        last = w_parts(bank[(6 + d) % 8][:, 0:TOKENS], c, f % FPC * D_MODEL + d * P,
                                       ad_hi[:, at:at + TOKENS], ad_lo[:, at:at + TOKENS], f == 0, f == FB - 1)
                        if f == FB - 1:
                            last.then_inc(proj_ready, 1)
                    if f < FB - 1:
                        last.then_inc(down_chunk, 1)
                return c0 + GROUPS

            pe.wait_ge(ones_ready, 1)
            pe.wait_ge(x_in, 32)
            large_ln("in", lambda b: None)
            c = mixer(0, 0)
            large_ln("mix0", lambda b: pe.wait_ge(r_ready, b + 1))
            c = dense(c)
            large_ln("ffn0", lambda b: pe.wait_ge(r_ready, KB + b + 1))
            c = mixer(1, c)
            large_ln("mix1", lambda b: pe.wait_ge(r_ready, 2 * KB + b + 1))

            pe.wait_ge(ln_out, LN_AT["mix1"] + KB)
            for t in range(TT):
                rows = TILE_ROWS[t]
                for k in range(KB):
                    last = mm(bank[0][0:rows, t * 8:t * 8 + 8], h[:, k, t * P:t * P + rows], w_router[:, k, :],
                              start=(k == 0), stop=(k == KB - 1))
            last.then_inc(logits_ready, 1)
            for t in range(TT):
                rows = TILE_ROWS[t]
                for half in range(2):
                    for k in range(4):
                        last = nc.tensor.transpose(bank[2 + 2 * t + half][0:rows, k * P:(k + 1) * P],
                                                   h[:, 4 * half + k, t * P:t * P + rows], ident)
                    last.then_inc(h_turned, 1)
            pe.wait_ge(chosen_ready, 1)
            for t in range(TT):
                for s in range(t + 1):
                    mm(bank[1][:, t * 8:t * 8 + 8], (before if s == t else ones)[:, :], chosen[:, s, :],
                       start=(s == 0), stop=(s == t))
            for s in range(TT):
                last = mm(bank[1][:, 24:32], ones[:, :], chosen[:, s, :], start=(s == 0), stop=(s == TT - 1))
            last.then_inc(pos_ready, 1)

            def gather(n, half):
                pe.wait_ge(sel_ready, n + 1)
                for k in range(4 * half, 4 * half + 4):
                    for t in range(TT):
                        rows = TILE_ROWS[t]
                        last = mm(bank[2 + half][:, k % 4 * W:(k % 4 + 1) * W],
                                  h_tok[0:rows, t, k * P:(k + 1) * P], sel[0:rows, t, :],
                                  start=(t == 0), stop=(t == TT - 1))
                last.then_inc(gathered, 1)

            def parts(out, hi, lo, w_at, columns, first, last):
                slot = w_at % SPLIT
                for n, (x, w) in enumerate(((hi, w_hi), (hi, w_lo), (lo, w_hi))):
                    ins = mm(out, x, w[slot][:, columns], start=(first and n == 0), stop=(last and n == 2),
                             skip_group_check=True)
                return ins

            pe.wait_ge(h_tok_dve, 3)
            pe.wait_ge(h_tok_act, 3)
            gather(0, 0)
            gather(0, 1)
            pe.sem_inc(chunk_done, SPLIT)
            pe.wait_ge(table_ready, 1)
            n_items = pe.value_load(table[0:1, 0:1], min_val=N_EXPERTS, max_val=N_EXPERTS + MAX_EXTRA)
            with pe.Fori(0, n_items) as i:
                def hidden(kind, g):
                    out = bank[2 * (g % 2) + (kind == "up")][:, 0:GC]
                    for half in range(2):
                        p = item_place[kind, g, half]
                        if kind == "gate" and g == 0:
                            pe.wait_ge(x_lo_done, i * 2 + half + 1)
                        pe.wait_ge(lo_done, i * CPI + START + p + 1)
                        for k in range(KB // 2):
                            kk = half * (KB // 2) + k
                            last = parts(out, x_hi[:, kk, 0:W], x_lo[:, kk, 0:W], START + p, slice(k * GC, (k + 1) * GC),
                                         kk == 0, kk == KB - 1)
                        last.then_inc(chunk_done, 1)

                def turn(g):
                    pe.wait_ge(e_act, i * E_GROUPS + g + 1)
                    for f in range(GB):
                        last = nc.tensor.transpose(bank[6][:, f * W:(f + 1) * W], gate_e[:, g % 2, f * P:(f + 1) * P],
                                                   ident)
                    last.then_inc(a_turned, 1)

                def down(g):
                    pe.wait_ge(a_lo_done, i * E_GROUPS + g + 1)
                    for half in range(2):
                        p = item_place["down", g, half]
                        pe.wait_ge(lo_done, i * CPI + START + p + 1)
                        for f in range(GB // 2):
                            ff = half * (GB // 2) + f
                            for d in range(2):
                                at = f * D_MODEL + d * 512
                                last = parts(bank[4 + d][:, :], a_hi[:, ff, :], a_lo[:, ff, :], START + p,
                                             slice(at, at + 512), g == 0 and ff == 0,
                                             g == E_GROUPS - 1 and ff == GB - 1)
                        last.then_inc(chunk_done, 1)

                hidden("gate", 0)
                pe.wait_ge(sel_w_ready, i + 1)
                pe.wait_ge(added, i * KB + KB)
                for t in range(TT):
                    rows = TILE_ROWS[t]
                    nc.tensor.transpose(bank[7][:, t * P:t * P + rows], sel[0:rows, t, :], ident[0:rows, 0:rows])
                for t in range(TT):
                    rows = TILE_ROWS[t]
                    last = mm(bank[7][:, TOKENS:TOKENS + 1], sel_w[0:rows, t, :], ones[0:rows, 0:1],
                              start=(t == 0), stop=(t == TT - 1))
                last.then_inc(sel_turned, 1)
                hidden("up", 0)
                for g in range(1, E_GROUPS):
                    if g >= 2:
                        pe.wait_ge(e_act, i * E_GROUPS + g - 1)
                    hidden("gate", g)
                    turn(g - 1)
                    hidden("up", g)
                    down(g - 1)
                turn(E_GROUPS - 1)
                gather(i + 1, 0)
                down(E_GROUPS - 1)
                gather(i + 1, 1)
                pe.wait_ge(scat_ready, i + 1)
                pe.wait_ge(x_lo_done, i * 2 + 3)
                for d in range(KB):
                    if d % 4 == 0:
                        pe.wait_ge(y_lo_done, i * 2 + d // 4 + 1)
                    if d == 6:
                        pe.wait_ge(x_lo_done, i * 2 + 4)
                    if d == 7:
                        pe.wait_ge(added, (i + 1) * KB + 1)
                    out = bank[SCATTER_BANKS[d]][:, 0:TOKENS]
                    mm(out, y_hi[:, d, :], scat[:, :], start=True, stop=False)
                    mm(out, y_lo[:, d, :], scat[:, :], start=False, stop=True).then_inc(scattered, 1)
            pe.wait_ge(added, n_items * KB + KB)
            large_ln("ffn1", lambda b: None)

        @block.scalar
        def _(act):
            A = nc.scalar.activation

            def v_at(name, layer, b):
                a = vec_at(name, layer) + b
                return vec[:, a:a + 1]

            def ln_squares(name, x, sq):
                for b in range(LN_BLOCKS[name]):
                    act.wait_ge(ln_xc, LN_AT[name] + b + 1)
                    A(sq[:, b, :], x[:, b, :], ACT.Square).then_inc(ln_sq, 1)

            def ln_gain(name, x, out, g, bias, func=ACT.Identity):
                for b in range(LN_BLOCKS[name]):
                    act.wait_ge(ln_xn, LN_AT[name] + b + 1)
                    A(out[:, b, :], x[:, b, :], func, scale=vec[:, g + b:g + b + 1],
                      bias=vec[:, bias + b:bias + b + 1]).then_inc(ln_out, 1)

            def z_out(layer, n, func, *outs):
                act.wait_ge(z_ready, 16 * layer + n + 1)
                b = bank[n % 6]
                if len(outs) == 1:
                    last = A(outs[0], b[:, 0:TOKENS], func)
                else:
                    A(outs[0], b[:, 0:SEQ], func)
                    last = A(outs[1], sample_cols(b), func)
                last.then_inc(z_act, 1)

            def cut(c):
                if c >= START:
                    item_arrived(act, 0, c - START)
                else:
                    arrived(act, c)
                if c >= SPLIT:
                    act.wait_ge(stream[c - SPLIT][1], stream[c - SPLIT][2])
                A(w_hi[c % SPLIT][:, :], ring[c % SLOTS][:, :], ACT.Copy).then_inc(hi_done, 1)

            def cut_rows(x, ks):
                for k in ks:
                    A(x_hi[:, k, :], x[:, k, :], ACT.Copy).then_inc(in_hi_done, 1)

            def mixer(layer, c0):
                for b in range(MB):
                    z_out(layer, b, ACT.Sigmoid, sig[:, b, :])
                cut(c0 + 3)
                cut(c0 + 4)
                for b in range(MB):
                    z_out(layer, 4 + b, ACT.Gelu, gv[:, b, :])
                cut(c0 + 5)
                for b in range(MB):
                    z_out(layer, 6 + b, ACT.Gelu, gu[:, b, :])
                cut(c0 + 6)
                if layer:
                    act.wait_ge(pool_step, 8)
                    act.wait_ge(st_d, 64)
                for b in range(MB):
                    z_out(layer, 8 + b, ACT.Copy, prompt_of(ext_d, b, POOL_PAST),
                          samples_of(ext_d, b, POOL_PAST, POOL_PAST, POOL_PAST + DEC_SEQ))
                cut(c0 + 7)
                ln_squares(f"v{layer}", gv, sq_s)
                for b in range(MB):
                    z_out(layer, 10 + b, ACT.Copy, cc[:, b, :])
                cut(c0 + 8)
                ln_gain(f"v{layer}", gv, vn, vec_at("ln_v_g", layer), vec_at("ln_v_b", layer))
                act.wait_ge(v_turned, 2 * layer + 1)
                A(v_tok[:, 0:2, :], bank[6][:, :].rearrange("p (t n) -> p t n", t=2), ACT.Copy).then_inc(v_tok_act, 1)
                act.wait_ge(v_turned, 2 * layer + 2)
                A(v_tok[0:N_SAMPLE, 2, :], bank[7][0:N_SAMPLE, 0:MB * P], ACT.Copy).then_inc(v_tok_act, 1)
                cut(c0 + 9)
                cut(c0 + 10)
                act.wait_ge(summed_s, 2 * MB * (layer + 1))
                for b in range(MB):
                    act.wait_ge(mapped_d, 2 * layer + b + 1)
                    A(y[:, 6 + b, :], bank[4 + b][:, 0:TOKENS], ACT.Copy,
                      scale=v_at("pool_scale", layer, b)).then_inc(y_d, 1)
                act.wait_ge(y_d, 2 * (layer + 1))
                cut_rows(y, [6, 7])
                ln_squares(f"a{layer}", acc_a, sq_s)
                act.wait_ge(z_dve, len(Z_BY_DVE) * (layer + 1))
                cut_rows(y, [4, 5])
                act.wait_ge(y_b, 2 * (layer + 1))
                cut_rows(y, [2, 3])
                ln_gain(f"a{layer}", acc_a, y, vec_at("ln_a_g", layer), vec_at("ln_a_b", layer), ACT.Silu)
                act.wait_ge(ln_out, LN_AT[f"a{layer}"] + MB)
                cut_rows(y, [0, 1])
                for c in range(c0 + 11, c0 + 15):
                    if c < START + CUT_AHEAD:
                        cut(c)

            def large_ln(name, g, bias, cut_after=False):
                x = h if name == "in" else r
                ln_squares(name, x, sq_l)
                if name == "in":
                    cut(0)
                    cut(1)
                for b in range(KB):
                    act.wait_ge(ln_xn, LN_AT[name] + b + 1)
                    A(h[:, b, :], x[:, b, :], ACT.Identity, scale=vec[:, g + b:g + b + 1],
                      bias=vec[:, bias + b:bias + b + 1]).then_inc(ln_out, 1)
                    if cut_after and b:
                        act.wait_ge(ln_out, LN_AT[name] + b)
                        cut_rows(h, [b - 1])
                if cut_after:
                    act.wait_ge(ln_out, LN_AT[name] + KB)
                    cut_rows(h, [KB - 1])

            for layer in range(DEPTH):
                nc.scalar.dma_start(ws_t[:, layer, :, :], t_in["ws_t"][layer].rearrange("h j i -> j h i")).then_inc(par_in, 16)
                nc.scalar.dma_start(ws_s[:, layer, :, :], t_in["ws_s"][layer].rearrange("h j i -> j h i")).then_inc(par_in, 16)
                nc.scalar.dma_start(bs[:, layer, :, :], t_in["bs_t"][layer].rearrange("(k p) t -> p k t", p=P)).then_inc(par_in, 16)
            nc.scalar.dma_start(w_router[:, :, :], t_in["w_router"][0].rearrange("(k p) e -> p k e", p=P)).then_inc(par_in, 16)
            act.wait_ge(vec_in, 16)
            large_ln("in", vec_at("ln_in_g"), vec_at("ln_in_b"), True)
            cut(2)
            mixer(0, 0)
            large_ln("mix0", vec_at("ln_mix_g", 0), vec_at("ln_mix_b", 0), True)
            for g in range(GROUPS):
                for f in range(FPC * g, FPC * (g + 1)):
                    act.wait_ge(gate_ready, f + 1)
                    if f >= 2:
                        act.wait_ge(act_done, f - 1)
                    A(gate_d[:, f % 2, :], bank[2 * (f % 3)][:, 0:TOKENS], ACT.Silu).then_inc(silu_done, 1)
                cut(DENSE_AT + 2 * g + 3)
                cut(DENSE_AT + 2 * g + 4)
            for g in range(GROUPS):
                for f in range(FPC * g, FPC * (g + 1)):
                    act.wait_ge(act_done, f + 1)
                    if f >= 2:
                        act.wait_ge(down_chunk, f - 1)
                    A(ad_hi[:, f % 2 * TOKENS:(f % 2 + 1) * TOKENS], act_d[:, f, :], ACT.Copy).then_inc(act_hi_done, 1)
                if g:
                    cut(DOWN_AT + g + 2)
            cut(DOWN_AT + GROUPS + 2)
            large_ln("ffn0", vec_at("ln_ffn_g", 0), vec_at("ln_ffn_b", 0), True)
            mixer(1, DOWN_AT + GROUPS)
            large_ln("mix1", vec_at("ln_mix_g", 1), vec_at("ln_mix_b", 1))

            act.wait_ge(st_v, 128)
            for t in range(TT):
                rows = TILE_ROWS[t]
                act.wait_ge(h_turned, 2 * t + 2)
                A(h_tok[0:rows, t, 512:1024], bank[3 + 2 * t][0:rows, :], ACT.Copy).then_inc(h_tok_act, 1)
            act.wait_ge(route, 5)
            A(col[:, 2, :], col[:, 2, :], ACT.Exp).then_inc(exp_done, 1)

            def tokens_hi(n, half):
                act.wait_ge(gathered, n * 2 + half + 1)
                A(x_hi[:, 4 * half:4 * half + 4, 0:W], bank[2 + half][:, :].rearrange("p (k n) -> p k n", k=4),
                  ACT.Copy).then_inc(x_hi_done, 1)

            tokens_hi(0, 0)
            tokens_hi(0, 1)
            act.wait_ge(table_ready, 1)
            n_items = act.value_load(table[0:1, 0:1], min_val=N_EXPERTS, max_val=N_EXPERTS + MAX_EXTRA)
            with act.Fori(0, n_items) as i:
                for p in range(CPI + 1):
                    for kind, g in before_split(p):
                        if kind == "silu":
                            act.wait_ge(chunk_done, i * CPI + SPLIT + item_place["gate", g, 1] + 1)
                            if g >= 2:
                                act.wait_ge(a_turned, i * E_GROUPS + g - 1)
                            A(gate_e[:, g % 2, :], bank[2 * (g % 2)][:, :], ACT.Silu).then_inc(e_silu, 1)
                        if kind == "parts":
                            act.wait_ge(a_turned, i * E_GROUPS + g + 1)
                            A(a_hi, bank[6][:, :].rearrange("p (f n) -> p f n", f=GB),
                              ACT.Copy).then_inc(a_hi_done, 1)
                        if kind == "act" and g == 0:
                            act.wait_ge(sel_turned, i + 1)
                            A(scat[:, :], bank[7][:, 0:TOKENS], ACT.Copy)
                            A(slot_gate[:, :], bank[7][:, TOKENS:TOKENS + 1], ACT.Copy).then_inc(scat_ready, 1)
                    if CUT_AHEAD <= p < CPI:
                        item_arrived(act, i, p)
                        act.wait_ge(chunk_done, i * CPI + p + 1)
                        A(w_hi[(START + p) % SPLIT][:, :], ring[(START + p) % SLOTS][:, :], ACT.Copy).then_inc(hi_done, 1)
                tokens_hi(i + 1, 0)
                with act.If(i < n_items - 1):
                    for p in range(CUT_AHEAD):
                        item_arrived(act, i + 1, p)
                        act.wait_ge(chunk_done, i * CPI + CPI + p + 1)
                        A(w_hi[(START + p) % SPLIT][:, :], ring[(START + p) % SLOTS][:, :], ACT.Copy).then_inc(hi_done, 1)
                act.wait_ge(chunk_done, i * CPI + SPLIT + CPI)
                act.wait_ge(scat_ready, i + 1)
                for half in range(2):
                    A(y_hi[:, 4 * half:4 * half + 4, :], bank[4 + half][:, :].rearrange("p (k n) -> p k n", k=4),
                      ACT.Copy, scale=slot_gate[:, 0:1]).then_inc(y_hi_done, 1)
                tokens_hi(i + 1, 1)
            large_ln("ffn1", vec_at("ln_ffn_g", 1), vec_at("ln_ffn_b", 1))

        @block.vector
        def _(dve):
            V = nc.vector

            def v_at(name, layer, b):
                a = vec_at(name, layer) + b
                return vec[:, a:a + 1]

            def ln_centre(name, x):
                dve.wait_ge(ln_mean, LNS.index(name) + 1)
                for b in range(LN_BLOCKS[name]):
                    V.tensor_tensor(x[:, b, :], x[:, b, :], bank[6][:, 0:TOKENS], ALU.subtract).then_inc(ln_xc, 1)

            def cut(c):
                dve.wait_ge(hi_done, c + 1)
                if c:
                    dve.wait_ge(lo_done, c)
                V.tensor_tensor(w_lo[c % SPLIT][:, :], ring[c % SLOTS][:, :], w_hi[c % SPLIT][:, :].bitcast(F32),
                                ALU.subtract).then_inc(lo_done, 1)

            def cut_one(x, stage, j, k):
                dve.wait_ge(in_hi_done, in_cuts(stage) + j + 1)
                V.tensor_tensor(x_lo[:, k, :], x[:, k, :], x_hi[:, k, :].bitcast(F32),
                                ALU.subtract).then_inc(in_lo_done, 1)

            def cut_rows(x, stage, order):
                for j, k in enumerate(order):
                    cut_one(x, stage, j, k)

            def ln_variance(name):
                n = LNS.index(name)
                dve.wait_ge(ln_var, n + 1)
                diag = diag_l if LN_BLOCKS[name] == KB else diag_s
                for t in range(TT):
                    rows = TILE_ROWS[t]
                    last = V.tensor_tensor_reduce(out=diag[0:rows, t, 0:rows], in0=bank[7][0:rows, t * P:t * P + rows],
                                                  in1=ident[0:rows, 0:rows], scale=1.0, scalar=LN_EPS, op0=ALU.mult,
                                                  op1=ALU.add, accum_out=var_tok[0:rows, t:t + 1])
                last.then_inc(ln_ve, 1)

            def ln_scale(name, x):
                dve.wait_ge(ln_spread, LNS.index(name) + 1)
                for b in range(LN_BLOCKS[name]):
                    V.tensor_tensor(x[:, b, :], x[:, b, :], bank[7][:, 0:TOKENS], ALU.mult).then_inc(ln_xn, 1)

            def residual(use, cuts={}):
                for d in range(KB):
                    dve.wait_ge(proj_ready, KB * use + d + 1)
                    V.scalar_tensor_tensor(out=r[:, d, :], in0=h[:, d, :], scalar=ALPHA,
                                           in1=bank[(6 + d) % 8][:, 0:TOKENS], op0=ALU.mult,
                                           op1=ALU.add).then_inc(r_ready, 1)
                    if d in cuts:
                        cut(cuts[d])

            def mixer(layer, c0):
                if layer:
                    dve.wait_ge(st_a, 64)
                for b in range(MB):
                    n = 2 + b
                    dve.wait_ge(z_ready, 16 * layer + n + 1)
                    dve.wait_ge(z_act, 10 * layer + b + 1)
                    V.tensor_tensor(prompt_of(ext_a, b, PAST_A), bank[n % 6][:, 0:SEQ], sig[:, b, 0:SEQ], ALU.mult)
                    V.tensor_tensor(samples_of(ext_a, b, PAST_A, PAST_A, PAST_A + DEC_SEQ),
                                    sample_cols(bank[n % 6]), sample_cols(sig[:, b, :]),
                                    ALU.mult).then_inc(z_dve, 1)
                cut(c0 + 3)
                cut(c0 + 4)

                def gated():
                    dve.wait_ge(past_c, 64 * (layer + 1))
                    if layer:
                        dve.wait_ge(st_c, 64)
                    for b in range(MB):
                        n = 12 + b
                        dve.wait_ge(z_ready, 16 * layer + n + 1)
                        dve.wait_ge(z_act, 10 * layer + 9 + b)
                        V.tensor_tensor(prompt_of(ext_c, b, PAST_C), bank[n % 6][:, 0:SEQ], cc[:, b, 0:SEQ], ALU.mult)
                        V.tensor_tensor(samples_of(ext_c, b, PAST_C, PAST_C, PAST_C + DEC_SEQ),
                                        sample_cols(bank[n % 6]), sample_cols(cc[:, b, :]),
                                        ALU.mult).then_inc(z_dve, 1)

                def samples_sum():
                    for b in range(MB):
                        dve.wait_ge(prods, MB * layer + b + 1)
                        V.tensor_reduce(sample_cols(acc_a[:, b, :]), prod_s[b], AX_X, ALU.add).then_inc(summed_s, 1)
                    for b in range(MB):
                        dve.wait_ge(summed_s, 2 * MB * layer + b + 1)
                        V.tensor_scalar(sample_cols(acc_a[:, b, :]), sample_cols(acc_a[:, b, :]),
                                        v_at("conv_a_b", layer, b), None, ALU.add).then_inc(summed_s, 1)

                between = {10: lambda: ln_centre(f"v{layer}", gv),
                           12: lambda: cut(c0 + 7), 15: lambda: ln_variance(f"v{layer}"),
                           18: lambda: cut(c0 + 8), 20: lambda: ln_scale(f"v{layer}", gv), 22: samples_sum,
                           26: gated}
                dve.wait_ge(z_dve, 6 * layer + 2)
                steps = MB * TAPS_A * layer
                for tap in range(TAPS_A):
                    if tap in between:
                        between[tap]()
                    for b in range(MB):
                        w = v_at("conv_a_w", layer, tap * MB + b)
                        src, out = ext_a[:, b, tap:tap + SEQ], acc_a[:, b, 0:SEQ]
                        if tap == 0:
                            V.tensor_scalar(out, src, w, v_at("conv_a_b", layer, b), ALU.mult,
                                            ALU.add).then_inc(conv_a, 1)
                        else:
                            dve.wait_ge(conv_a, steps - 1)
                            V.scalar_tensor_tensor(out=out, in0=src, scalar=w, in1=out, op0=ALU.mult,
                                                   op1=ALU.add).then_inc(conv_a, 1)
                        steps += 1
                n_out = LEN_C - PAST_C
                for tap in range(TAPS_C):
                    for b in range(MB):
                        w = v_at("conv_c_w", layer, tap * MB + b)
                        src, out = ext_c[:, b, tap:tap + n_out], acc_c[:, b, 0:n_out]
                        if tap == 0:
                            dve.wait_ge(z_dve, 6 * layer + 3 + b)
                            V.tensor_scalar(out, src, w, None, ALU.mult).then_inc(conv_c, 1)
                        else:
                            dve.wait_ge(conv_c, 6 * layer + 2 * (tap - 1) + b + 1)
                            V.scalar_tensor_tensor(out=out, in0=src, scalar=w, in1=out, op0=ALU.mult,
                                                   op1=ALU.add).then_inc(conv_c, 1)
                ln_centre(f"a{layer}", acc_a)
                for b in range(MB):
                    n = 14 + b
                    dve.wait_ge(z_ready, 16 * layer + n + 1)
                    dve.wait_ge(conv_c, 6 * layer + 5 + b)
                    V.tensor_tensor(y[:, 4 + b, 0:SEQ], bank[n % 6][:, 0:SEQ], acc_c[:, b, 0:SEQ], ALU.mult)
                    rows = acc_c[:, b, SEQ + PAST_C:LEN_C].rearrange("p (s l) -> p s l", s=DEC_BATCH)[:, :, 0:DEC_SEQ]
                    V.tensor_tensor(sample_cols(y[:, 4 + b, :]), sample_cols(bank[n % 6]), rows,
                                    ALU.mult).then_inc(z_dve, 1)
                cut_rows(y, f"y{layer}", Y_ORDER[:4])
                dve.wait_ge(par_in, PARAMS * 16)
                for b in range(MB):
                    dve.wait_ge(mixed_b, 2 * layer + b + 1)
                    V.tensor_tensor(cc[:, b, :], bank[b][:, 0:TOKENS], bs[:, layer, b, :], ALU.add).then_inc(b_sum, 1)
                    dve.wait_ge(b_sum, 2 * layer + b + 1)
                    V.tensor_tensor(y[:, 2 + b, :], cc[:, b, :], gu[:, b, :], ALU.mult).then_inc(y_b, 1)
                ln_variance(f"a{layer}")
                for j in range(4, 6):
                    cut_one(y, f"y{layer}", j, Y_ORDER[j])
                ln_scale(f"a{layer}", acc_a)
                for j in range(6, 8):
                    cut_one(y, f"y{layer}", j, Y_ORDER[j])

            V.memset(ones_model[:, :], 1.0 / D_MODEL)
            V.memset(minus_half[:, :], -0.5)
            V.memset(var_tok[:, :], 1.0)
            V.memset(ones_mix[:, :], 1.0 / (MB * P))
            V.memset(ones[:, :], 1.0).then_inc(ones_ready, 1)
            V.memset(ext_a[:, :, 0:PAST_A], 0.0)
            V.memset(ext_c[:, :, 0:PAST_C], 0.0)
            V.memset(ext_d[:, :, 0:POOL_PAST], 0.0)
            V.memset(sum_a[:, :, 0:1], 0.0).then_inc(ones_ready, 1)
            ln_centre("in", h)
            dve.wait_ge(cst_in, 16)
            cut(0)
            cut(1)
            ln_variance("in")
            ln_scale("in", h)
            cut_rows(h, "in", range(KB))
            cut(2)
            dve.wait_ge(vec_in, 16)
            mixer(0, 0)
            n = len(Z_CHUNKS)
            residual(0, {1: n + 3, 3: DENSE_AT, 5: DENSE_AT + 1})
            ln_centre("mix0", r)
            cut(DENSE_AT + 2)
            ln_variance("mix0")
            ln_scale("mix0", r)
            cut_rows(h, "mix0", range(KB))
            dve.wait_ge(st_v, 64)
            for g in range(GROUPS):
                for f in range(FPC * g, FPC * (g + 1)):
                    dve.wait_ge(silu_done, f + 1)
                    dve.wait_ge(up_ready, f + 1)
                    V.tensor_tensor(act_d[:, f, :], gate_d[:, f % 2, :], bank[2 * (f % 3) + 1][:, 0:TOKENS],
                                    ALU.mult).then_inc(act_done, 1)
                    cut(DENSE_AT + 3 + f)
            for g in range(GROUPS):
                for f in range(FPC * g, FPC * (g + 1)):
                    dve.wait_ge(act_hi_done, f + 1)
                    at = f % 2 * TOKENS
                    V.tensor_tensor(ad_lo[:, at:at + TOKENS], act_d[:, f, :], ad_hi[:, at:at + TOKENS].bitcast(F32),
                                    ALU.subtract).then_inc(act_lo_done, 1)
                if g:
                    cut(DOWN_AT + g + 2)
            residual(1)
            ln_centre("ffn0", r)
            cut(DOWN_AT + GROUPS + 2)
            ln_variance("ffn0")
            ln_scale("ffn0", r)
            cut_rows(h, "ffn0", range(KB))
            mixer(1, DOWN_AT + GROUPS)
            residual(2, {1: START - 1, 3: START, 5: START + 1})
            ln_centre("mix1", r)
            ln_variance("mix1")
            ln_scale("mix1", r)

            steps = [0]

            def step(ins):
                steps[0] += 1
                ins.then_inc(route, 1)
                dve.wait_ge(route, steps[0])

            def over_experts(v):
                return v.unsqueeze(2).broadcast_to([P, TT, N_EXPERTS])

            rank8 = const("rank8").unsqueeze(1).broadcast_to([P, TT, N_EXPERTS])
            dve.wait_ge(ln_out, LN_AT["mix1"] + KB)
            dve.wait_ge(st_v, 128)
            step(V.memset(logit[:, :, :], 0.0))
            dve.wait_ge(logits_ready, 1)
            V.tensor_copy(logit[:, 0:2, :], bank[0][:, 0:16].rearrange("p (t e) -> p t e", t=2))
            V.tensor_copy(logit[0:N_SAMPLE, 2, :], bank[0][0:N_SAMPLE, 16:24]).then_inc(route, 1)
            steps[0] += 1
            dve.wait_ge(route, steps[0])

            def top(values, hot, best):
                V.tensor_reduce(best, values, AX_X, ALU.max).then_inc(chosen_top, 1)
                tops[0] += 1
                dve.wait_ge(chosen_top, tops[0])
                for ins in (
                    lambda: V.tensor_tensor(key[:, :, :], values, over_experts(best), ALU.is_equal),
                    lambda: V.tensor_tensor(key[:, :, :], key[:, :, :], rank8, ALU.mult),
                    lambda: V.tensor_reduce(col[:, 7, :], key[:, :, :], AX_X, ALU.max),
                    lambda: V.tensor_tensor(hot, key[:, :, :], over_experts(col[:, 7, :]), ALU.is_equal),
                ):
                    ins().then_inc(chosen_top, 1)
                    tops[0] += 1
                    dve.wait_ge(chosen_top, tops[0])

            tops = [0]
            top(logit[:, :, :], hot1[:, :, :], col[:, 0, :])
            step(V.scalar_tensor_tensor(out=logit[:, :, :], in0=hot1[:, :, :], scalar=-3.0e38, in1=logit[:, :, :],
                                        op0=ALU.mult, op1=ALU.add))
            top(logit[:, :, :], hot2[:, :, :], col[:, 1, :])
            step(V.tensor_tensor(chosen[:, :, :], hot1[:, :, :], hot2[:, :, :], ALU.add))
            valid = over_experts(const("valid"))
            V.tensor_tensor(chosen[:, :, :], chosen[:, :, :], valid, ALU.mult).then_inc(chosen_ready, 1)
            for t in range(TT):
                dve.wait_ge(h_turned, 2 * t + 1)
                rows = TILE_ROWS[t]
                V.tensor_copy(h_tok[0:rows, t, 0:512], bank[2 + 2 * t][0:rows, :]).then_inc(h_tok_dve, 1)
            step(V.tensor_tensor(col[:, 2, :], col[:, 1, :], col[:, 0, :], ALU.subtract))
            dve.wait_ge(pos_ready, 1)
            dve.wait_ge(chosen_ready, 1)
            item_p = item_pos[:, :, 0:N_EXPERTS]
            step(V.scalar_tensor_tensor(out=item_p, in0=bank[1][:, 0:24].rearrange("p (t e) -> p t e", t=TT),
                                        scalar=1.0, in1=chosen[:, :, :], op0=ALU.add, op1=ALU.mult))
            step(V.tensor_scalar(item_p, item_p, -1.0, None, ALU.add))

            def select(dst, column, ready):
                for t in range(TT):
                    rows = TILE_ROWS[t]
                    last = V.tensor_scalar(dst[0:rows, t, :], const("slot")[0:rows, :], item_pos[0:rows, t, column],
                                           None, ALU.is_equal)
                last.then_inc(ready, 1)

            select(sel, slice(0, 1), sel_ready)
            dve.wait_ge(exp_done, 1)
            step(V.tensor_scalar(col[:, 3, :], col[:, 2, :], 1.0, None, ALU.add))
            step(V.reciprocal(col[:, 4, :], col[:, 3, :]))
            step(V.tensor_tensor(col[:, 5, :], col[:, 4, :], col[:, 2, :], ALU.mult))
            item_g = item_gate[:, :, 0:N_EXPERTS]
            step(V.tensor_tensor(item_g, hot1[:, :, :], over_experts(col[:, 4, :]), ALU.mult))
            step(V.tensor_tensor(hot2[:, :, :], hot2[:, :, :], over_experts(col[:, 5, :]), ALU.mult))
            step(V.tensor_tensor(item_g, item_g, hot2[:, :, :], ALU.add))
            step(V.tensor_copy(counts[:, :], bank[1][:, 24:32]))
            for m in range(LEVELS):
                a = m * N_EXPERTS
                V.tensor_scalar(is_extra[:, a:a + N_EXPERTS], counts[:, :], float((m + 1) * W), None, ALU.is_gt)
                V.tensor_scalar(cand_pos[:, :, a:a + N_EXPERTS], item_p, -float((m + 1) * W), None, ALU.add)
                step(V.tensor_copy(cand_gate[:, :, a:a + N_EXPERTS], item_g))
            square = tmp[:, 0:CAND * CAND].rearrange("p (a b) -> p a b", a=CAND)
            step(V.tensor_tensor(square, const("earlier", CAND),
                                 is_extra[:, :].unsqueeze(1).broadcast_to([P, CAND, CAND]), ALU.mult))
            step(V.tensor_reduce(extra_rank[:, :], square, AX_X, ALU.add))
            step(V.tensor_tensor(picked[:, :, :], extra_rank[:, :].unsqueeze(1).broadcast_to([P, MAX_EXTRA, CAND]),
                                 const("extra_no").unsqueeze(2).broadcast_to([P, MAX_EXTRA, CAND]), ALU.is_equal))
            step(V.tensor_tensor(picked[:, :, :], picked[:, :, :],
                                 is_extra[:, :].unsqueeze(1).broadcast_to([P, MAX_EXTRA, CAND]), ALU.mult))
            for src, dst in ((cand_pos, item_pos), (cand_gate, item_gate)):
                for t in range(TT):
                    prod = tmp[:, 0:MAX_EXTRA * CAND].rearrange("p (a b) -> p a b", a=MAX_EXTRA)
                    step(V.tensor_tensor(prod, picked[:, :, :],
                                         src[:, t, :].unsqueeze(1).broadcast_to([P, MAX_EXTRA, CAND]), ALU.mult))
                    step(V.tensor_reduce(dst[:, t, N_EXPERTS:N_EXPERTS + MAX_EXTRA], prod, AX_X, ALU.add))
                step(V.memset(dst[:, :, N_ITEMS - 1:N_ITEMS], 0.0))
            prod = tmp[:, 0:MAX_EXTRA * CAND].rearrange("p (a b) -> p a b", a=MAX_EXTRA)
            step(V.tensor_tensor(prod, picked[:, :, :],
                                 const("cand_expert").unsqueeze(1).broadcast_to([P, MAX_EXTRA, CAND]), ALU.mult))
            step(V.tensor_reduce(tab_f[:, 1:1 + MAX_EXTRA], prod, AX_X, ALU.add))
            step(V.tensor_reduce(tab_f[:, 0:1], is_extra[:, :], AX_X, ALU.add))
            step(V.tensor_scalar(tab_f[:, 0:1], tab_f[:, 0:1], float(N_EXPERTS), None, ALU.add))
            V.tensor_copy(table[0:1, :], tab_f[0:1, :]).then_inc(table_ready, 1)
            for d in range(KB):
                V.tensor_scalar(r[:, d, :], h[:, d, :], ALPHA, None, ALU.mult).then_inc(added, 1)
            dve.wait_ge(table_ready, 1)
            dve.wait_ge(gathered, 1)

            def tokens_lo(n, half):
                dve.wait_ge(x_hi_done, n * 2 + half + 1)
                V.tensor_tensor(x_lo[:, 4 * half:4 * half + 4, 0:W], bank[2 + half][:, :].rearrange("p (k n) -> p k n", k=4),
                                x_hi[:, 4 * half:4 * half + 4, 0:W].bitcast(F32), ALU.subtract).then_inc(x_lo_done, 1)

            tokens_lo(0, 0)
            tokens_lo(0, 1)
            n_items = dve.value_load(table[0:1, 0:1], min_val=N_EXPERTS, max_val=N_EXPERTS + MAX_EXTRA)
            with dve.Fori(0, n_items) as i:
                for t in range(TT):
                    rows = TILE_ROWS[t]
                    last = V.tensor_scalar(sel_w[0:rows, t, :], const("slot")[0:rows, :],
                                           item_pos[0:rows, t, bass.ds(i, 1)], item_gate[0:rows, t, bass.ds(i, 1)],
                                           ALU.is_equal, ALU.mult)
                last.then_inc(sel_w_ready, 1)
                for p in range(CPI + 1):
                    for kind, g in before_split(p):
                        if kind == "act":
                            dve.wait_ge(e_silu, i * E_GROUPS + g + 1)
                            dve.wait_ge(chunk_done, i * CPI + SPLIT + item_place["up", g, 1] + 1)
                            V.tensor_tensor(gate_e[:, g % 2, :], gate_e[:, g % 2, :], bank[2 * (g % 2) + 1][:, :],
                                            ALU.mult).then_inc(e_act, 1)
                            if g == 3:
                                select(sel, bass.ds(i + 1, 1), sel_ready)
                        if kind == "parts":
                            dve.wait_ge(a_hi_done, i * E_GROUPS + g + 1)
                            V.tensor_tensor(a_lo, bank[6][:, :].rearrange("p (f n) -> p f n", f=GB),
                                            a_hi.bitcast(F32), ALU.subtract).then_inc(a_lo_done, 1)
                    if CUT_AHEAD <= p < CPI:
                        dve.wait_ge(hi_done, i * CPI + START + p + 1)
                        V.tensor_tensor(w_lo[(START + p) % SPLIT][:, :], ring[(START + p) % SLOTS][:, :],
                                        w_hi[(START + p) % SPLIT][:, :].bitcast(F32), ALU.subtract).then_inc(lo_done, 1)
                tokens_lo(i + 1, 0)

                def cut_next(p):
                    with dve.If(i < n_items - 1):
                        dve.wait_ge(hi_done, i * CPI + CPI + START + p + 1)
                        V.tensor_tensor(w_lo[(START + p) % SPLIT][:, :], ring[(START + p) % SLOTS][:, :],
                                        w_hi[(START + p) % SPLIT][:, :].bitcast(F32), ALU.subtract).then_inc(lo_done, 1)

                cut_next(0)
                cut_next(1)
                for half in range(2):
                    dve.wait_ge(y_hi_done, i * 2 + half + 1)
                    V.scalar_tensor_tensor(out=y_lo[:, 4 * half:4 * half + 4, :],
                                           in0=bank[4 + half][:, :].rearrange("p (k n) -> p k n", k=4),
                                           scalar=slot_gate[:, 0:1],
                                           in1=y_hi[:, 4 * half:4 * half + 4, :].bitcast(F32), op0=ALU.mult,
                                           op1=ALU.subtract).then_inc(y_lo_done, 1)
                tokens_lo(i + 1, 1)
                for d in range(KB):
                    dve.wait_ge(scattered, i * KB + d + 1)
                    V.tensor_tensor(r[:, d, :], r[:, d, :], bank[SCATTER_BANKS[d]][:, 0:TOKENS],
                                    ALU.add).then_inc(added, 1)
            ln_centre("ffn1", r)
            ln_variance("ffn1")
            ln_scale("ffn1", r)

        @block.gpsimd
        def _(pool):
            G = nc.gpsimd

            def layer_norm_root(name):
                n = LNS.index(name)
                pool.wait_ge(ln_ve, n + 1)
                G.tensor_tensor(rstd_tok[:, :], var_tok[:, :], minus_half[:, :], ALU.pow).then_inc(ln_rs, 1)

            G.memset(w_pool[:, :, :, :], 0.0).then_inc(pool_set, 1)
            pool.wait_ge(pool_set, 1)
            for layer in range(DEPTH):
                for half in range(2):
                    lo = 64 * half
                    G.dma_start(w_pool[lo:lo + 64, layer, :, lo:lo + 64],
                                t_in["w_pool"][layer].rearrange("(b two) c d -> two c b d", two=2)[half]).then_inc(w_pool_in, 16)

            def load_past(layer):
                for ext, past, src, done in ((ext_a, PAST_A, "past_a", past_a), (ext_c, PAST_C, "past_c", past_c),
                                             (ext_d, POOL_PAST, "past_d", past_d)):
                    for b in range(MB):
                        v = samples_of(ext, b, past, 0, past)
                        s = t_in[src][layer, b * P:(b + 1) * P]
                        for half in range(2):
                            lo = 4 * half
                            G.dma_start(v[:, lo:lo + 4, :], s[:, lo:lo + 4, :]).then_inc(done, 16)

            load_past(0)
            pool.wait_ge(ones_ready, 2)
            layer_norm_root("in")
            pool.wait_ge(par_in, PARAMS * 16)
            for layer in range(DEPTH):
                G.affine_select(out=ws_t[:, layer, :, :], in_=ws_t[:, layer, :, :], compare_op=ALU.is_ge, fill=0.0,
                                base=0, pattern=[[0, HEADS], [1, CHUNK]], channel_multiplier=-1)
            w4 = ws_s[:, :, :, :].rearrange("p l h i -> p (l h) i")
            G.affine_select(out=w4, in_=w4, compare_op=ALU.is_ge, fill=0.0, base=0,
                            pattern=[[0, DEPTH * HEADS], [1, N_SAMPLE]], channel_multiplier=-1).then_inc(pool_set, 1)
            pool.wait_ge(pool_set, 2)
            w5 = ws_s[:, :, :, :].rearrange("p l h (s i) -> p (l h) s i", s=DEC_BATCH)
            G.affine_select(out=w5, in_=w5, compare_op=ALU.is_ge, fill=0.0, base=0,
                            pattern=[[0, DEPTH * HEADS], [-DEC_SEQ, DEC_BATCH], [0, DEC_SEQ]],
                            channel_multiplier=1).then_inc(setup, 1)

            def pooling(layer):
                base = 8 * layer
                pool.wait_ge(past_d, 64 * (layer + 1))
                pool.wait_ge(z_act, 10 * layer + 8)
                n = LEN_D

                def add(dst, src, p0, b0, shift, lo):
                    return G.tensor_tensor(dst[p0:P, b0:MB, lo:n], src[p0:P, b0:MB, lo:n],
                                           src[p0:P, b0:MB, lo - shift:n - shift], ALU.add)

                add(sum_a, ext_d, 0, 0, 1, 1).then_inc(pool_step, 1)
                pool.wait_ge(pool_step, base + 1)
                add(sum_b, sum_a, 0, 0, 2, 3).then_inc(pool_step, 1)
                layer_norm_root(f"v{layer}")
                pool.wait_ge(pool_step, base + 2)
                add(sum_a, sum_b, 0, 1, 4, 7).then_inc(pool_step, 1)
                pool.wait_ge(pool_step, base + 3)
                add(sum_b, sum_a, 64, 1, 8, 15).then_inc(pool_step, 1)
                pool.wait_ge(pool_step, base + 4)
                inv = const("inv_count", MB)
                for lo, s in ((0, sum_a), (64, sum_b)):
                    hi = lo + 64
                    G.tensor_tensor(dd[lo:hi, :, 0:SEQ], s[lo:hi, :, POOL_PAST:POOL_PAST + SEQ],
                                    inv[lo:hi, :, 0:SEQ], ALU.mult)
                    for b in range(MB):
                        last = G.tensor_tensor(sample_cols(dd[:, b, :])[lo:hi],
                                               samples_of(s, b, POOL_PAST, POOL_PAST, POOL_PAST + DEC_SEQ)[lo:hi],
                                               sample_cols(inv[:, b, :])[lo:hi], ALU.mult)
                    last.then_inc(pool_step, 1)
                pool.wait_ge(pool_step, base + 6)
                G.tensor_tensor(dd[:, :, 0:SEQ], dd[:, :, 0:SEQ], ext_d[:, :, POOL_PAST:POOL_PAST + SEQ],
                                ALU.subtract).then_inc(pool_step, 1)
                for b in range(MB):
                    last = G.tensor_tensor(sample_cols(dd[:, b, :]), sample_cols(dd[:, b, :]),
                                           samples_of(ext_d, b, POOL_PAST, POOL_PAST, POOL_PAST + DEC_SEQ), ALU.subtract)
                last.then_inc(pool_step, 1)

            def store_rows(layer, ext, past, name, done):
                for b in range(MB):
                    G.dma_start(t_out[name + "_p"][layer, b * P:(b + 1) * P], ext[:, b, SEQ:SEQ + past]).then_inc(done, 16)
                    G.dma_start(t_out[name + "_s"][layer, b * P:(b + 1) * P],
                                samples_of(ext, b, past, DEC_SEQ, DEC_SEQ + past)).then_inc(done, 16)

            def cut(c):
                pool.wait_ge(hi_done, c + 1)
                pool.wait_ge(lo_done, c)
                G.tensor_tensor(w_lo[c % SPLIT][:, :], ring[c % SLOTS][:, :], w_hi[c % SPLIT][:, :].bitcast(F32),
                                ALU.subtract).then_inc(lo_done, 1)

            pool.wait_ge(cst_in, 16)
            pool.wait_ge(ones_ready, 2)
            for layer in range(DEPTH):
                pool.wait_ge(past_a, 64 * (layer + 1))
                pool.wait_ge(z_dve, 6 * layer + 2)
                at = vec_at("conv_a_w", layer)
                for b in range(MB):
                    taps = vec[:, at + b:at + b + MB * (TAPS_A - 1) + 1:MB]
                    for l in range(DEC_SEQ):
                        last = G.tensor_tensor(prod_s[b][:, :, l, :], samples_of(ext_a, b, PAST_A, l, l + TAPS_A),
                                               taps.unsqueeze(1).broadcast_to([P, DEC_BATCH, TAPS_A]), ALU.mult)
                    last.then_inc(prods, 1)
                c0 = DOWN_AT + GROUPS if layer else 0
                cut(c0 + 5)
                cut(c0 + 6)
                pooling(layer)
                cut(c0 + 9)
                cut(c0 + 10)
                layer_norm_root(f"a{layer}")
                store_rows(layer, ext_a, PAST_A, "conv_a", st_a)
                store_rows(layer, ext_d, POOL_PAST, "pool_d", st_d)
                pool.wait_ge(z_dve, 6 * layer + 4)
                store_rows(layer, ext_c, PAST_C, "conv_c", st_c)
                pool.wait_ge(ln_out, LN_AT[f"v{layer}"] + MB)
                for b in range(MB):
                    G.dma_start(t_out["v_p"][layer, b * P:(b + 1) * P], vn[:, b, SEQ - CHUNK:SEQ]).then_inc(st_v, 16)
                    G.dma_start(t_out["v_s"][layer, b * P:(b + 1) * P], vn[:, b, SEQ:TOKENS]).then_inc(st_v, 16)
                if layer + 1 < DEPTH:
                    pool.wait_ge(z_dve, 6 * layer + 6)
                    for s in (st_a, st_c, st_d):
                        pool.wait_ge(s, 64 * (layer + 1))
                    load_past(layer + 1)
                layer_norm_root(f"mix{layer}")
                layer_norm_root(f"ffn{layer}")
            for s in (st_a, st_c, st_d, st_v):
                pool.wait_ge(s, 64 * DEPTH)


PARAMS = 3 * DEPTH + 1

_OUTS = {"y_t": (D_MODEL, TOKENS), "conv_a_p": (DEPTH, MB * P, PAST_A), "conv_a_s": (DEPTH, MB * P, DEC_BATCH, PAST_A),
         "conv_c_p": (DEPTH, MB * P, PAST_C), "conv_c_s": (DEPTH, MB * P, DEC_BATCH, PAST_C),
         "pool_d_p": (DEPTH, MB * P, POOL_PAST), "pool_d_s": (DEPTH, MB * P, DEC_BATCH, POOL_PAST),
         "v_p": (DEPTH, MB * P, CHUNK), "v_s": (DEPTH, MB * P, N_SAMPLE)}


def constants():
    c = {}
    c["ident"] = np.eye(P)
    c["before"] = np.triu(np.ones((P, P)), 1)
    window = np.array([2, 4, 8, 16]).repeat(64).reshape(MB, P).T
    pos = np.concatenate([np.arange(SEQ), np.full(N_SAMPLE, SEQ)])
    c["inv_count"] = 1.0 / np.minimum(pos[None, None, :] + 1.0, window[:, :, None])
    c["slot"] = np.tile(np.arange(W), (P, 1))
    c["rank8"] = np.tile(N_EXPERTS - np.arange(N_EXPERTS), (P, 1))
    c["valid"] = np.stack([np.arange(P) < n for n in TILE_ROWS], 1)
    c["extra_no"] = np.tile(np.arange(MAX_EXTRA), (P, 1))
    c["earlier"] = np.tile(np.tril(np.ones((CAND, CAND)), -1).reshape(-1), (P, 1))
    c["cand_expert"] = np.tile(np.arange(CAND) % N_EXPERTS, (P, 1))
    return np.concatenate([c[n].reshape(P, size) for n, size in CST], axis=1).astype(np.float32)


def kernel(**inputs):
    import concourse.bacc as _bacc
    from concourse.bass_utils import run_bass_kernel_spmd as _run

    x = {k: np.asarray(v) for k, v in inputs.items()}
    arrays = {"cst": constants()}
    rows = np.concatenate([x["x_prompt"].reshape(SEQ, D_MODEL), x["x_sample"].reshape(N_SAMPLE, D_MODEL)])
    arrays["x_t"] = rows.T
    vecs = [x["ln_in_g"].reshape(-1, P), x["ln_in_b"].reshape(-1, P)]
    for layer in range(DEPTH):
        vecs += [x[name][layer].reshape(-1, P) for name, _ in VEC]
    arrays["vec"] = np.concatenate(vecs).T
    for name, src in (("past_a", "state_conv_a"), ("past_c", "state_conv_c"), ("past_d", "state_pool_d")):
        arrays[name] = x[src].transpose(0, 3, 1, 2)
    arrays["ws_t"] = x["w_s"].transpose(0, 1, 3, 2)
    arrays["ws_s"] = np.tile(x["w_s"][:, :, :DEC_SEQ, :DEC_SEQ].transpose(0, 1, 3, 2), (1, 1, DEC_BATCH, DEC_BATCH))
    bias = np.concatenate([x["b_s"], x["b_s"], np.tile(x["b_s"][:, :, :DEC_SEQ], (1, 1, DEC_BATCH))], axis=2)
    arrays["bs_t"] = bias.repeat(MB * P // HEADS, axis=1)
    for name in ("w_in", "w_out", "w_pool", "w_router", "w_ff_gate", "w_ff_up", "w_ff_down", "w_e_gate", "w_e_up", "w_e_down"):
        arrays[name] = x[name]

    nc = _bacc.Bacc("TRN2", target_bir_lowering=False, num_devices=1)
    arrays = {f"in_{k}": np.ascontiguousarray(v) for k, v in arrays.items()}
    t_in = {k[3:]: nc.dram_tensor(k, v.shape, F32, kind="ExternalInput").ap() for k, v in arrays.items()}
    t_out = {k: nc.dram_tensor(f"out_{k}", s, F32, kind="ExternalOutput").ap() for k, s in _OUTS.items()}
    build(nc, t_in, t_out)
    got = _run(nc, [arrays], core_ids=[0]).results[0]

    y = got["out_y_t"].T
    y_prompt = y[:SEQ].reshape(1, SEQ, D_MODEL)
    y_sample = y[SEQ:].reshape(DEC_BATCH, DEC_SEQ, D_MODEL)

    def prompt_rows(name):
        return got[f"out_{name}_p"].transpose(0, 2, 1)[:, None]

    def sample_rows(name):
        return got[f"out_{name}_s"].transpose(0, 2, 3, 1)

    v_s = got["out_v_s"].transpose(0, 2, 1).reshape(DEPTH, DEC_BATCH, DEC_SEQ, MB * P)
    out = (y_prompt, y_sample, prompt_rows("conv_a"), prompt_rows("conv_c"), prompt_rows("pool_d"), prompt_rows("v"),
           sample_rows("conv_a"), sample_rows("conv_c"), sample_rows("pool_d"), v_s)
    return tuple(np.ascontiguousarray(o) for o in out)
```
